# Optimizing a Trainium2 kernel written in Bass

```python
import math
import jax
import jax.numpy as jnp
from jax import lax
import numpy as np

D_MODEL = 1024
BATCH = 1
SEQ = 1024
DEPTH = 1

N_META = 16
RMS_EPS = 1e-6
ATT_HEADS = 8
ATT_QK_DIM = 64
ATT_V_DIM = 2 * ATT_QK_DIM
ATT_QK_WIDTH = 2 * ATT_HEADS * ATT_QK_DIM
ATT_V_WIDTH = ATT_HEADS * ATT_V_DIM
SUBLN_EPS = 1e-5
ROPE_THETA = 10000.0
Q_BLOCK = 128
RWKV_HEAD = 64
RWKV_WIDTH = D_MODEL
RWKV_HEADS = RWKV_WIDTH // RWKV_HEAD
DECAY_LORA = 64
AAA_LORA = 64
GATE_LORA = 160
RWKV_COLS = 3 * RWKV_WIDTH + DECAY_LORA + AAA_LORA + GATE_LORA
RWKV_SPLITS = (RWKV_WIDTH, 2 * RWKV_WIDTH, 3 * RWKV_WIDTH, 3 * RWKV_WIDTH + DECAY_LORA,
               3 * RWKV_WIDTH + DECAY_LORA + AAA_LORA)
LNX_EPS = 64e-5
IN_SPLITS = (ATT_QK_WIDTH, 2 * ATT_QK_WIDTH, 2 * ATT_QK_WIDTH + ATT_V_WIDTH,
             2 * ATT_QK_WIDTH + ATT_V_WIDTH + RWKV_COLS)
IN_COLS = IN_SPLITS[-1] + 2 * D_MODEL
FFN_HIDDEN = -(-8 * D_MODEL // (3 * 256)) * 256

kernel_name = 'gated_diffattn_birwkv7_swiglu_encoder_layer'

def _rms_norm(x, g, eps=RMS_EPS):
    xf = x.astype(jnp.float32)
    y = xf * lax.rsqrt(jnp.mean(xf * xf, axis=-1, keepdims=True) + eps)
    return (y * g.astype(jnp.float32)).astype(x.dtype)

def _rope(x, pos):
    d = x.shape[-1]
    inv = 1.0 / (ROPE_THETA ** (jnp.arange(0, d, 2, dtype=jnp.float32) / d))
    ang = pos.astype(jnp.float32)[:, None] * inv[None, :]
    cos = jnp.cos(ang)[None, :, None, :]
    sin = jnp.sin(ang)[None, :, None, :]
    xf = x.astype(jnp.float32)
    x1, x2 = xf[..., : d // 2], xf[..., d // 2:]
    return jnp.concatenate([x1 * cos - x2 * sin, x2 * cos + x1 * sin], axis=-1).astype(x.dtype)

def _centred_shift_mix(p, mu):
    prev = jnp.pad(p[:, :-1], ((0, 0), (1, 0), (0, 0)))
    nxt = jnp.pad(p[:, 1:], ((0, 0), (0, 1), (0, 0)))
    return p + mu * (0.5 * (prev + nxt) - p)

def _diff_attention(q, k, v, pos, lq1, lk1, lq2, lk2, subln_g, lambda_init):
    B, T, _ = q.shape
    H, dq, dv = ATT_HEADS, ATT_QK_DIM, ATT_V_DIM
    f32 = jnp.float32
    q = _rope(q.reshape(B, T, 2 * H, dq), pos)
    k = _rope(k.reshape(B, T, 2 * H, dq), pos)
    v = v.reshape(B, T, H, dv)
    lam = (jnp.exp(jnp.sum(lq1.astype(f32) * lk1.astype(f32)))
           - jnp.exp(jnp.sum(lq2.astype(f32) * lk2.astype(f32))) + lambda_init)
    n_blk = -(-T // Q_BLOCK)
    qp = jnp.pad(q, ((0, 0), (0, n_blk * Q_BLOCK - T), (0, 0), (0, 0)))
    qb = qp.reshape(B, n_blk, Q_BLOCK, 2 * H, dq).transpose(1, 0, 3, 2, 4)
    kt = k.transpose(0, 2, 1, 3)
    vt = v.transpose(0, 2, 1, 3)
    scale = dq ** -0.5

    def one_block(qblk):
        s = jnp.einsum('bnqd,bnkd->bnqk', qblk, kt).astype(f32) * scale
        p = jax.nn.softmax(s, axis=-1).reshape(B, H, 2, Q_BLOCK, T)
        p = p[:, :, 0] - lam * p[:, :, 1]
        return jnp.einsum('bhqk,bhkd->bhqd', p.astype(vt.dtype), vt)

    o = lax.map(one_block, qb)
    o = o.transpose(1, 0, 3, 2, 4).reshape(B, n_blk * Q_BLOCK, H, dv)[:, :T]
    o = _rms_norm(o, subln_g, SUBLN_EPS) * (1.0 - lambda_init)
    return o.reshape(B, T, H * dv)

def _rwkv7_bidirectional(p, w0, w_up, a0, a_up, g_up, k_k, k_a, r_k, lnx_g, lnx_b):
    f32 = jnp.float32
    out_dtype = p.dtype
    B, T, _ = p.shape
    H, N, C = RWKV_HEADS, RWKV_HEAD, RWKV_WIDTH
    p = p.astype(f32)
    r, k, v, xw, xa, xg = jnp.split(p, RWKV_SPLITS, axis=-1)
    w_log = -jax.nn.softplus(-(w0.astype(f32)[:, None, None, :]
                               + jnp.einsum('btl,zlc->zbtc', jnp.tanh(xw), w_up.astype(f32)))) - 0.5
    decay = jnp.exp(-jnp.exp(w_log))
    a = jax.nn.sigmoid(a0.astype(f32)[:, None, None, :]
                       + jnp.einsum('btl,zlc->zbtc', xa, a_up.astype(f32)))
    g = jnp.einsum('btl,lc->btc', jax.nn.sigmoid(xg), g_up.astype(f32))
    hd = lambda t: t.reshape(t.shape[:-1] + (H, N))
    kk = hd(k * k_k.astype(f32))
    kk = kk / jnp.maximum(jnp.sqrt(jnp.sum(kk * kk, axis=-1, keepdims=True)), 1e-12)
    k_dir = hd(k[None] * (1.0 + (a - 1.0) * k_a.astype(f32)))
    a_h = hd(a)
    r_h, v_h = hd(r), hd(v)
    two = lambda t: jnp.broadcast_to(t[None], (2,) + t.shape)

    def time_major(t):
        t = jnp.stack([t[0], jnp.flip(t[1], axis=1)])
        return jnp.moveaxis(t, 2, 0)

    inputs = (time_major(two(r_h)), time_major(hd(decay)), time_major(k_dir),
              time_major(two(v_h)), time_major(two(-kk)), time_major(kk[None] * a_h))

    def step(S, inp):
        r_t, w_t, k_t, v_t, a_t, b_t = inp
        sa = jnp.einsum('zbhvk,zbhk->zbhv', S, a_t)
        S = S * w_t[..., None, :] + sa[..., None] * b_t[..., None, :] + v_t[..., None] * k_t[..., None, :]
        return S, jnp.einsum('zbhvk,zbhk->zbhv', S, r_t)

    S0 = jnp.zeros((2, B, H, N, N), f32)
    _, ys = lax.scan(step, S0, inputs)
    ys = jnp.moveaxis(ys, 0, 2)
    y = ys[0] + jnp.flip(ys[1], axis=1)
    mean = jnp.mean(y, axis=-1, keepdims=True)
    var = jnp.mean((y - mean) ** 2, axis=-1, keepdims=True)
    y = ((y - mean) * lax.rsqrt(var + LNX_EPS)).reshape(B, T, C)
    y = y * lnx_g.astype(f32) + lnx_b.astype(f32)
    bonus = jnp.einsum('bthn,zbthn,hn->bth', r_h, k_dir, r_k.astype(f32))[..., None] * v_h
    return ((y + bonus.reshape(B, T, C)) * g).astype(out_dtype)

def setup_inputs(seed: int = 0) -> dict:
    key = jax.random.key(seed)
    ks = jax.random.split(key, 32)
    L, D, C, H, N, F = DEPTH, D_MODEL, RWKV_WIDTH, RWKV_HEADS, RWKV_HEAD, FFN_HIDDEN
    f32 = jnp.float32
    nrm = lambda k, shape, s: jax.random.normal(k, shape, f32) * s
    gain = lambda k, shape: 1.0 + 0.05 * jax.random.normal(k, shape, f32)
    return {
        'x': nrm(ks[0], (BATCH, SEQ, D), 1.0),
        'meta_tokens': nrm(ks[1], (N_META, D), 1.0),
        'pre_mix_g': gain(ks[2], (L, D)),
        'w_in': nrm(ks[3], (L, D, IN_COLS), D ** -0.5),
        'att_lq1': nrm(ks[4], (L, ATT_QK_DIM), 0.1),
        'att_lk1': nrm(ks[5], (L, ATT_QK_DIM), 0.1),
        'att_lq2': nrm(ks[6], (L, ATT_QK_DIM), 0.1),
        'att_lk2': nrm(ks[7], (L, ATT_QK_DIM), 0.1),
        'att_subln_g': gain(ks[8], (L, ATT_V_DIM)),
        'rwkv_mu': jax.random.uniform(ks[9], (L, RWKV_COLS), f32),
        'rwkv_w0': jax.random.uniform(ks[10], (L, 2, C), f32, -4.0, 1.0),
        'rwkv_w_up': nrm(ks[11], (L, 2, DECAY_LORA, C), 0.05),
        'rwkv_a0': nrm(ks[12], (L, 2, C), 0.3),
        'rwkv_a_up': nrm(ks[13], (L, 2, AAA_LORA, C), 0.05),
        'rwkv_g_up': nrm(ks[14], (L, GATE_LORA, C), GATE_LORA ** -0.5),
        'rwkv_k_k': 0.85 + 0.05 * jax.random.normal(ks[15], (L, C), f32),
        'rwkv_k_a': gain(ks[16], (L, C)),
        'rwkv_r_k': nrm(ks[17], (L, H, N), 0.1),
        'rwkv_lnx_g': gain(ks[18], (L, C)),
        'rwkv_lnx_b': nrm(ks[19], (L, C), 0.01),
        'w_out': nrm(ks[20], (L, D, D), D ** -0.5),
        'post_mix_g': gain(ks[21], (L, D)),
        'pre_ffn_g': gain(ks[22], (L, D)),
        'w_ffn_in': nrm(ks[23], (L, D, 2 * F), D ** -0.5),
        'w_ffn_out': nrm(ks[24], (L, F, D), F ** -0.5),
        'post_ffn_g': gain(ks[25], (L, D)),
    }

def reference(x, meta_tokens, pre_mix_g, w_in, att_lq1, att_lk1, att_lq2, att_lk2, att_subln_g,
              rwkv_mu, rwkv_w0, rwkv_w_up, rwkv_a0, rwkv_a_up, rwkv_g_up, rwkv_k_k, rwkv_k_a,
              rwkv_r_k, rwkv_lnx_g, rwkv_lnx_b, w_out, post_mix_g, pre_ffn_g, w_ffn_in, w_ffn_out,
              post_ffn_g):
    B = x.shape[0]
    meta = jnp.broadcast_to(meta_tokens[None].astype(x.dtype), (B, N_META, D_MODEL))
    h = jnp.concatenate([meta, x], axis=1)
    T = h.shape[1]
    pos = jnp.arange(T, dtype=jnp.int32)
    for layer in range(DEPTH):
        lambda_init = 0.8 - 0.6 * math.exp(-0.3 * layer)
        u = _rms_norm(h, pre_mix_g[layer])
        proj = jnp.einsum('btd,dp->btp', u, w_in[layer])
        q, k, v, rw, gates = jnp.split(proj, IN_SPLITS, axis=-1)
        att = _diff_attention(q, k, v, pos, att_lq1[layer], att_lk1[layer], att_lq2[layer],
                              att_lk2[layer], att_subln_g[layer], lambda_init)
        rw = _centred_shift_mix(rw, rwkv_mu[layer])
        rwk = _rwkv7_bidirectional(rw, rwkv_w0[layer], rwkv_w_up[layer], rwkv_a0[layer],
                                   rwkv_a_up[layer], rwkv_g_up[layer], rwkv_k_k[layer],
                                   rwkv_k_a[layer], rwkv_r_k[layer], rwkv_lnx_g[layer],
                                   rwkv_lnx_b[layer])
        gate_a, gate_r = jnp.split(gates, 2, axis=-1)
        merged = jax.nn.sigmoid(gate_a) * att + jax.nn.sigmoid(gate_r) * rwk
        mix = jnp.einsum('btc,cd->btd', merged, w_out[layer])
        h = h + _rms_norm(mix, post_mix_g[layer])
        u = _rms_norm(h, pre_ffn_g[layer])
        gu = jnp.einsum('btd,df->btf', u, w_ffn_in[layer])
        g_ff, up = jnp.split(gu, 2, axis=-1)
        f = jnp.einsum('btf,fd->btd', jax.nn.silu(g_ff) * up, w_ffn_out[layer])
        h = h + _rms_norm(f, post_ffn_g[layer])
    return h[:, N_META:]


_drawn_inputs = setup_inputs


def setup_inputs(seed=0):
    import zlib

    import numpy as np

    out = dict(_drawn_inputs(seed))
    spreads = {}
    factors = {'att_lq2': 2.778,
     'rwkv_w_up': 3.972,
     'rwkv_k_k': 70.078,
     'rwkv_lnx_g': 7.244,
     'rwkv_lnx_b': 33.476,
     'att_lk1': 4.364,
     'att_subln_g': 2.694}
    for name, (base, spread) in spreads.items():
        noise = np.random.default_rng([zlib.crc32(name.encode()), seed]).standard_normal(out[name].shape)
        drawn = base * np.exp(spread * noise) if base else spread * noise
        out[name] = jnp.asarray(drawn.astype(out[name].dtype))
    for name, factor in factors.items():
        out[name] = (out[name] * factor).astype(out[name].dtype)
    return out
```

```python
import math
from contextlib import ExitStack

import numpy as np

import concourse.bass as bass
from concourse import mybir

F32 = mybir.dt.float32
ALU = mybir.AluOpType
ACT = mybir.ActivationFunctionType
AX = mybir.AxisListType.X

P = 128
D = 1024
KC = D // P
META = 16
SEQ = 1024
T = SEQ + META
EPS = 1e-6

L = 104
NT = T // L
NB = 4
NW = T // NB

HEADS = 8
DQ = 64
N = 64
RW0 = 3 * D
LORA0 = RW0 + 3 * D
GL = 160
GATE0 = LORA0 + 2 * N + GL
COLS = GATE0 + 2 * D
DECAY = math.exp(-0.5)

PAR = {}
for _name, _n in (("mu", 24), ("mu_lora", 3), ("w0", 16), ("a0", 16), ("k_k", 8), ("k_a", 8), ("r_k", 8),
                  ("lnx_g", 8), ("lnx_b", 8), ("pre_mix_g", 8), ("post_mix_g", 8), ("pre_ffn_g", 8),
                  ("post_ffn_g", 8), ("subln_g", 1)):
    PAR[_name] = sum(n for _, n in PAR.values()), _n
NPAR = sum(n for _, n in PAR.values())


def par(name, i=0):
    return bass.ds(PAR[name][0] + i, 1)

FFN = 2816
FT = FFN // P


def cols(bank_tile):
    return bank_tile[:, :, 0:NW]


def banked(ap):
    return ap.rearrange("p (n w) -> p n w", n=NB)


class Chain:

    def __init__(self, eng, sem, first=0):
        self.eng, self.sem, self.first, self.n = eng, sem, first, 0

    def __call__(self, ins):
        self.n += 1
        ins.then_inc(self.sem, 1)
        self.eng.wait_ge(self.sem, self.first + self.n)


def norm_and_turn(nc, sems, meta, x, ident, table, uT):
    with ExitStack() as ctx:
        sb = lambda n, s: ctx.enter_context(nc.sbuf_tensor(n, s, F32))
        sem = lambda n: sems.enter_context(nc.semaphore(n))
        xt = [sb(f"n1_x{s}", [L, D]) for s in range(2)]
        un = [sb(f"n1_u{s}", [L, D]) for s in range(2)]
        sq = sb("n1_sq", [L, D])
        ms = [sb(f"n1_ms{s}", [L, 4]) for s in range(2)]
        eps = sb("n1_eps", [P, 1])
        ps = ctx.enter_context(nc.psum_tensor("n1_ps", [P, 2, 2, 512], F32))
        eps_set = sem("n1_eps_set")
        x_in = [sem(f"n1_x_in{s}") for s in range(2)]
        summed = sem("n1_summed")
        rooted = sem("n1_rooted")
        chain = sem("n1_chain")
        normed = sem("n1_normed")
        u_turned = sem("n1_u_turned")
        u_kept = sem("n1_u_kept")

        def turned(s, half):
            return ps[:, s, half, 0:4 * L].rearrange("p (k t) -> p k t", k=4)

        with nc.Block() as block:
            @block.sync
            def _(sp):
                sp.sem_inc(x_in[1], 16)
                for t in range(NT):
                    s = t % 2
                    if t >= 2:
                        sp.wait_ge(normed, t - 1)
                    if t == 0:
                        sp.dma_start(xt[0][0:META, :], meta).then_inc(x_in[0], 16)
                        sp.dma_start(xt[0][META:L, :], x[0:L - META, :]).then_inc(x_in[0], 16)
                    else:
                        sp.dma_start(xt[s][:], x[t * L - META:(t + 1) * L - META, :]).then_inc(x_in[s], 16)

            @block.scalar
            def _(act):
                act.wait_ge(eps_set, 1)
                with act.Fori(0, NT // 2) as i:
                    for s in range(2):
                        act.wait_ge(x_in[s], 16 * i + 32)
                        nc.scalar.activation(sq[:], xt[s][:], ACT.Square,
                                             accum_out=ms[s][:, 0:1]).then_inc(summed, 1)
                        act.wait_ge(summed, 2 * i + s + 1)
                        nc.scalar.activation(ms[s][:, 1:2], ms[s][:, 0:1], ACT.Sqrt, bias=eps[0:L, :],
                                             scale=1.0 / D).then_inc(rooted, 1)

            @block.vector
            def _(dve):
                nc.vector.memset(eps[:], EPS).then_inc(eps_set, 1)
                with dve.Fori(0, NT // 2) as i:
                    for s in range(2):
                        dve.wait_ge(rooted, 2 * i + s + 1)
                        nc.vector.reciprocal(ms[s][:, 2:3], ms[s][:, 1:2]).then_inc(chain, 1)
                        dve.wait_ge(chain, 2 * i + s + 1)
                        dve.wait_ge(u_turned, 2 * i + s + 1)
                        nc.vector.tensor_scalar(un[s][:], xt[s][:], ms[s][:, 2:3], None,
                                                ALU.mult).then_inc(normed, 1)
                        dve.wait_ge(u_turned, 2 * i + s + 3)
                        for half in range(2):
                            out = uT[:, 4 * half:4 * half + 4, bass.ts(2 * i + s, L)]
                            gb = table[:, PAR["pre_mix_g"][0] + 4 * half:PAR["pre_mix_g"][0] + 4 * half + 4].unsqueeze(2).broadcast_to([P, 4, L])
                            nc.vector.tensor_tensor(out, turned(s, half), gb, ALU.mult).then_inc(u_kept, 1)

            @block.tensor
            def _(pe):
                pe.sem_inc(u_turned, 2)
                pe.sem_inc(u_kept, 4)
                with pe.Fori(0, NT // 2) as i:
                    for s in range(2):
                        pe.wait_ge(normed, 2 * i + s + 1)
                        pe.wait_ge(u_kept, 4 * i + 2 * s + 2)
                        for k in range(KC):
                            ins = nc.tensor.transpose(turned(s, k // 4)[:, k % 4, :],
                                                      un[s][:, k * P:(k + 1) * P], ident[0:L, 0:L])
                        ins.then_inc(u_turned, 1)



def load_constants(nc, sems, ident_d, ones_d, table_d, ident, ones, table, more):
    here = sems.enter_context(nc.semaphore("c_here"))
    done = sems.enter_context(nc.semaphore("c_done"))
    with nc.Block() as block:
        @block.sync
        def _(sp):
            sp.dma_start(ident[:], ident_d).then_inc(here, 16)
            sp.dma_start(ones[:], ones_d).then_inc(here, 16)
            sp.dma_start(table[:], table_d).then_inc(here, 16)

        @block.vector
        def _(dve):
            dve.wait_ge(here, 48)
            mu = table[:, 0:27]
            nc.vector.tensor_scalar(more[:, 0:27], mu, -1.0, 1.0, ALU.mult, ALU.add).then_inc(done, 1)
            nc.vector.tensor_scalar(more[:, 27:54], mu, 0.5, None, ALU.mult).then_inc(done, 1)
            nc.vector.tensor_scalar(more[:, 54:86], table[:, 27:59], 0.5, None, ALU.mult).then_inc(done, 1)
            k_a = table[:, PAR["k_a"][0]:PAR["k_a"][0] + 8]
            nc.vector.tensor_scalar(more[:, 86:94], k_a, -1.0, 1.0, ALU.mult, ALU.add).then_inc(done, 1)
            dve.wait_ge(done, 4)


def keep(i):
    return bass.ds(i, 1)


def half_mu(i):
    return bass.ds(27 + i, 1)


def half_bias(i):
    return bass.ds(54 + i, 1)


def one_minus_ka(i):
    return bass.ds(86 + i, 1)


def low_rank_inputs(nc, sems, w_lora, uT, more, lor, gl, gl2):
    with ExitStack() as ctx:
        sb = lambda n, s: ctx.enter_context(nc.sbuf_tensor(n, s, F32))
        sem = lambda n: sems.enter_context(nc.semaphore(n))
        W = 2 * N + GL
        w = sb("lr_w", [P, KC, W])
        raw = [sb(f"lr_raw{j}", [P, T + 2]) for j in range(3)]
        kept = [sb(f"lr_kept{j}", [P, T]) for j in range(3)]
        shifted = [sb(f"lr_shifted{j}", [P, T]) for j in range(3)]
        ps = [ctx.enter_context(nc.psum_tensor(f"lr_ps{s}", [P, NB, 512], F32)) for s in range(2)]
        w_here, product, copied, padded = sem("lr_w_here"), sem("lr_product"), sem("lr_copied"), sem("lr_padded")
        scaled, summed, mixed, done = sem("lr_scaled"), sem("lr_summed"), sem("lr_mixed"), sem("lr_done")
        rows = [P, P, GL - P]
        out = [lor, gl, gl2]

        with nc.Block() as block:
            @block.sync
            def _(sp):
                sp.dma_start(w[:], w_lora).then_inc(w_here, 16)

            @block.tensor
            def _(pe):
                pe.wait_ge(w_here, 16)
                for j, m in enumerate(rows):
                    if j == 2:
                        pe.wait_ge(scaled, 1)
                    for n in range(NB):
                        for k in range(KC):
                            ins = nc.tensor.matmul(ps[j % 2][0:m, n, 0:NW], w[:, k, j * P:j * P + m],
                                                   uT[:, k, n * NW:(n + 1) * NW], start=(k == 0), stop=(k == KC - 1))
                    ins.then_inc(product, 1)

            @block.scalar
            def _(act):
                for j, m in enumerate(rows):
                    act.wait_ge(product, j + 1)
                    nc.scalar.copy(banked(raw[j][0:m, 1:T + 1]), ps[j % 2][0:m, :, 0:NW]).then_inc(copied, 1)
                    nc.scalar.activation(banked(kept[j][0:m, :]), ps[j % 2][0:m, :, 0:NW], ACT.Copy,
                                         scale=more[0:m, keep(24 + j)]).then_inc(scaled, 1)
                act.wait_ge(mixed, 1)
                nc.scalar.activation(lor[0:N, :], lor[0:N, :], ACT.Tanh).then_inc(done, 1)
                act.wait_ge(mixed, 3)
                nc.scalar.activation(gl[:], gl[:], ACT.Sigmoid).then_inc(done, 1)
                nc.scalar.activation(gl2[0:GL - P, :], gl2[0:GL - P, :], ACT.Sigmoid).then_inc(done, 1)
                act.wait_ge(done, 3)

            @block.vector
            def _(dve):
                for j in range(3):
                    nc.vector.memset(raw[j][:, 0:1], 0.0).then_inc(padded, 1)
                    nc.vector.memset(raw[j][:, T + 1:T + 2], 0.0).then_inc(padded, 1)
                dve.wait_ge(padded, 6)
                for j, m in enumerate(rows):
                    dve.wait_ge(copied, j + 1)
                    nc.vector.tensor_tensor(shifted[j][0:m, :], raw[j][0:m, 0:T], raw[j][0:m, 2:T + 2],
                                            ALU.add).then_inc(summed, 1)
                    dve.wait_ge(summed, j + 1)
                    dve.wait_ge(scaled, j + 1)
                    nc.vector.scalar_tensor_tensor(out[j][0:m, :], shifted[j][0:m, :], more[0:m, half_mu(24 + j)],
                                                   kept[j][0:m, :], ALU.mult, ALU.add).then_inc(mixed, 1)


TURNS = ["r", "k", "v", "w0", "w1", "a0", "a1", "g", "att_q", "att_k", "kk_sum", "bonus", "att_v", "gate_a", "gate_r"]
MAIN = ["r", "k", "v", "att_q", "att_k", "att_v", "gate_a", "gate_r"]
PER = [sum(1 for t in range(len(TURNS)) if t % 2 == s) for s in range(2)]
REC_AT = {"log0": 0, "kd0": L + 1, "nb0": 2 * L + 1, "r": 3 * L + 1, "v": 4 * L + 1, "kk": 5 * L + 1,
          "kd1": 6 * L + 1, "nb1": 7 * L + 1, "log1": 8 * L + 1}
REC = 9 * L + 2
HALF_REC = 6 * L + 1
KEPT = ["att_q", "att_k", "att_v", "gate_a", "gate_r", "g", "bonus_v"]


def project_and_prepare(nc, sems, w_main, w_low, uT, ones, table, more, lor, gl, gl2, prep_d, kept_d):
    with ExitStack() as ctx:
        sb = lambda n, s: ctx.enter_context(nc.sbuf_tensor(n, s, F32))
        sem = lambda n: sems.enter_context(nc.semaphore(n))
        wt = [sb(f"pp_w{s}", [P, KC, P]) for s in range(2)]
        wl = sb("pp_wl", [P, 6, P])
        raw = {x: sb(f"pp_raw_{x}", [P, T + 2]) for x in "rkv"}
        scaled = {x: sb(f"pp_scaled_{x}", [P, T]) for x in "rkv"}
        neighbours = sb("pp_neighbours", [P, T])
        th = [sb(f"pp_th{j}", [P, T]) for j in range(4)]
        kmix = sb("pp_kmix", [P, T])
        kk = sb("pp_kk", [P, T])
        sq = sb("pp_sq", [P, T])
        tmp = sb("pp_tmp", [P, T])
        rk = sb("pp_rk", [P, T])
        bv = sb("pp_bv", [P, T])
        ob = [sb(f"pp_ob{s}", [P, T]) for s in range(2)]
        sums = sb("pp_sums", [P, T])
        within = sb("pp_within", [P, T])
        prep = sb("pp_prep", [P, NT, REC])
        ps = [ctx.enter_context(nc.psum_tensor(f"pp_ps{s}", [P, NB, 512], F32)) for s in range(2)]

        filled = [sem(f"pp_filled{s}") for s in range(2)]
        emptied = [sem(f"pp_emptied{s}") for s in range(2)]
        w_here = [sem(f"pp_w_here{s}") for s in range(2)]
        wl_here = sem("pp_wl_here")
        padded, ready = sem("pp_padded"), sem("pp_ready")
        stored = [sem(f"pp_stored{s}") for s in range(2)]
        prep_stored = sem("pp_prep_stored")
        bonus_stored = sem("pp_bonus_stored")
        once = {}
        for name in ("raw_r", "raw_k", "raw_v", "summed_r", "summed_k", "summed_v", "mixed_r", "mixed_k", "mixed_v",
                     "kk_raw", "kk_squared", "lw_0", "lw_1", "log_sum_0", "log_sum_1", "log_0", "log_1", "log_first", "a_0", "a_1", "kf_0", "kf_1", "kd_0", "kd_1", "kd_both",
                     "rk", "kk_root", "kk_inverse", "kk_done", "b_0", "b_1", "bonus_done"):
            once[name] = sem(f"pp_{name}")
        before = lambda i: i + 1
        now = lambda i: i + 2

        def count(i, turn, s):
            return PER[s] * i + PER[s] + turn // 2 + 1

        def slot(name):
            turn = TURNS.index(name)
            return turn, turn % 2

        def out(name):
            return prep[:, :, REC_AT[name]:REC_AT[name] + L]

        by_chunk = lambda ap: ap.rearrange("p (c t) -> p c t", c=NT)

        with nc.Block() as block:
            @block.sync
            def _(sp):
                for name in once:
                    sp.sem_inc(once[name], 1)
                sp.sem_inc(prep_stored, 16)
                with sp.Fori(0, HEADS) as i:
                    sp.wait_ge(filled[1], count(i - 1, TURNS.index("g"), 1))
                    sp.dma_start(wl[:], w_low[i]).then_inc(wl_here, 16)
                    for j, name in enumerate(MAIN):
                        was, s = slot(MAIN[j - 2])
                        sp.wait_ge(filled[s], count(i - (j < 2), was, s))
                        sp.dma_start(wt[j % 2][:], w_main[i, j]).then_inc(w_here[j % 2], 16)
                    for done in ("mixed_r", "mixed_v", "log_0", "log_1", "log_first", "kd_0", "kd_1", "kk_done", "b_0",
                                 "b_1"):
                        sp.wait_ge(once[done], now(i))
                    sp.dma_start(prep_d[i].rearrange("c p a -> p c a"), prep[:]).then_inc(prep_stored, 16)
                sp.wait_ge(prep_stored, 16 * HEADS + 16)

            @block.tensor
            def _(pe):
                for s in range(2):
                    pe.sem_inc(filled[s], PER[s])
                with pe.Fori(0, HEADS) as i:
                    pe.wait_ge(wl_here, 16 * i + 16)
                    for turn, name in enumerate(TURNS):
                        s = turn % 2
                        pe.wait_ge(emptied[s], count(i, turn, s) - 1)
                        if name in MAIN:
                            j = MAIN.index(name)
                            pe.wait_ge(w_here[j % 2], 64 * i + 16 * (j // 2) + 16)
                            parts = [(wt[j % 2][:, k, :], uT[:, k, :]) for k in range(KC)]
                        elif name == "g":
                            parts = [(wl[:, 4, :], gl[:]), (wl[0:GL - P, 5, :], gl2[:])]
                        elif name == "kk_sum":
                            pe.wait_ge(once["kk_squared"], now(i))
                            parts = [(ones[:], sq[:])]
                        elif name == "bonus":
                            pe.wait_ge(once["rk"], now(i))
                            parts = [(ones[:], rk[:])]
                        else:
                            parts = [(wl[:, ["w0", "w1", "a0", "a1"].index(name), :], lor[:])]
                        for n in range(NB):
                            for k, (weights, moving) in enumerate(parts):
                                ins = nc.tensor.matmul(ps[s][:, n, 0:NW], weights, moving[:, n * NW:(n + 1) * NW],
                                                       start=(k == 0), stop=(k == len(parts) - 1))
                        ins.then_inc(filled[s], 1)

            @block.scalar
            def _(act):
                for s in range(2):
                    act.sem_inc(emptied[s], PER[s])
                    act.sem_inc(stored[s], 16)
                act.sem_inc(bonus_stored, 16)
                act.wait_ge(padded, 6)
                with act.Fori(0, HEADS) as i:
                    def fill(name):
                        turn, s = slot(name)
                        act.wait_ge(filled[s], count(i, turn, s))
                        return s

                    def take_mixed(x):
                        s = fill(x)
                        act.wait_ge(once[f"summed_{x}"], before(i))
                        nc.scalar.copy(banked(raw[x][:, 1:T + 1]), cols(ps[s])).then_inc(once[f"raw_{x}"], 1)
                        act.wait_ge(once[f"mixed_{x}"], before(i))
                        nc.scalar.activation(banked(scaled[x][:]), cols(ps[s]), ACT.Copy,
                                             scale=more[:, keep("rkv".index(x) * HEADS + i)]).then_inc(emptied[s], 1)

                    def keep_turn(name, n):
                        s = fill(name)
                        act.wait_ge(stored[n % 2], 48 * i + 16 * (n // 2) + 16)
                        func = ACT.Sigmoid if name.startswith("gate") else ACT.Copy
                        nc.scalar.activation(banked(ob[n % 2][:]), cols(ps[s]), func).then_inc(emptied[s], 1)
                        act.wait_ge(emptied[s], count(i, TURNS.index(name), s))
                        act.dma_start(kept_d[KEPT.index(name), i], ob[n % 2][:]).then_inc(stored[n % 2], 16)

                    for x in "rkv":
                        take_mixed(x)
                    act.wait_ge(once["mixed_k"], now(i))
                    act.wait_ge(once["kk_done"], before(i))
                    nc.scalar.activation(kk[:], kmix[:], ACT.Copy, scale=table[:, par("k_k", i)]).then_inc(once["kk_raw"], 1)
                    act.wait_ge(once["kk_raw"], now(i))
                    act.wait_ge(filled[0], count(i - 1, TURNS.index("kk_sum"), 0))
                    nc.scalar.activation(sq[:], kk[:], ACT.Square).then_inc(once["kk_squared"], 1)
                    for j, name in enumerate(("w0", "w1", "a0", "a1")):
                        s = fill(name)
                        act.wait_ge(once[("kd_0", "kd_1", "b_0", "b_1")[j]], before(i))
                        nc.scalar.activation(banked(th[j][:]), cols(ps[s]), ACT.Tanh, scale=0.5,
                                             bias=more[:, half_bias(8 * j + i)]).then_inc(emptied[s], 1)
                    keep_turn("g", 0)
                    keep_turn("att_q", 1)
                    keep_turn("att_k", 2)
                    s = fill("bonus")
                    act.wait_ge(bonus_stored, 16 * i + 16)
                    nc.scalar.copy(banked(bv[:]), cols(ps[s])).then_inc(emptied[s], 1)
                    act.wait_ge(emptied[0], count(i, TURNS.index("kk_sum"), 0))
                    nc.scalar.activation(tmp[:], tmp[:], ACT.Sqrt).then_inc(once["kk_root"], 1)
                    keep_turn("att_v", 3)
                    act.wait_ge(once["bonus_done"], now(i))
                    act.dma_start(kept_d[KEPT.index("bonus_v"), i], bv[:]).then_inc(bonus_stored, 16)
                    keep_turn("gate_a", 4)
                    keep_turn("gate_r", 5)
                for s in range(2):
                    act.wait_ge(stored[s], 48 * HEADS + 16)
                act.wait_ge(bonus_stored, 16 * HEADS + 16)

            @block.gpsimd
            def _(pool):
                for x in "rkv":
                    nc.gpsimd.memset(raw[x][:, 0:1], 0.0).then_inc(padded, 1)
                    nc.gpsimd.memset(raw[x][:, T + 1:T + 2], 0.0).then_inc(padded, 1)
                pool.wait_ge(padded, 6)
                with pool.Fori(0, HEADS) as i:
                    for n, x in enumerate("rkv"):
                        pool.wait_ge(once[f"raw_{x}"], now(i))
                        pool.wait_ge(once[f"mixed_{'vrk'[n]}"], now(i) - (n == 0))
                        nc.gpsimd.tensor_tensor(neighbours[:], raw[x][:, 0:T], raw[x][:, 2:T + 2],
                                                ALU.add).then_inc(once[f"summed_{x}"], 1)

            @block.vector
            def _(dve):
                nc.vector.memset(within[:], 1.0).then_inc(ready, 1)
                nc.vector.memset(prep[:, :, REC_AT["log0"]:REC_AT["log0"] + 1], 0.0).then_inc(ready, 1)
                dve.wait_ge(ready, 2)
                nc.vector.memset(by_chunk(within[:])[:, :, 0:1], 0.0).then_inc(ready, 1)
                dve.wait_ge(ready, 3)
                with dve.Fori(0, HEADS) as i:
                    def once_is(name):
                        dve.wait_ge(once[name], now(i))

                    def read(name):
                        turn, s = slot(name)
                        dve.wait_ge(emptied[s], count(i, turn, s))

                    dve.wait_ge(prep_stored, 16 * i + 16)
                    for n, (x, dst) in enumerate((("r", out("r")), ("k", by_chunk(kmix[:])), ("v", out("v")))):
                        once_is(f"summed_{x}")
                        read(x)
                        nc.vector.scalar_tensor_tensor(dst, by_chunk(neighbours[:]), more[:, half_mu(8 * n + i)],
                                                       by_chunk(scaled[x][:]), ALU.mult,
                                                       ALU.add).then_inc(once[f"mixed_{x}"], 1)
                    for z in range(2):
                        read(f"w{z}")
                        nc.vector.tensor_scalar(th[z][:], th[z][:], -0.5 * DECAY, -0.5 * DECAY,
                                                ALU.mult, ALU.add).then_inc(once[f"lw_{z}"], 1)
                        once_is(f"lw_{z}")
                        dve.wait_ge(once[f"log_{1 - z}"], now(i) - (z == 0))
                        nc.vector.tensor_tensor_scan(out=sums[:], data0=within[:], data1=th[z][:], initial=0.0,
                                                     op0=ALU.mult, op1=ALU.add).then_inc(once[f"log_sum_{z}"], 1)
                        once_is(f"log_sum_{z}")
                        if z == 0:
                            nc.vector.tensor_copy(prep[:, :, REC_AT["log0"] + 1:REC_AT["log0"] + 1 + L],
                                                  by_chunk(sums[:])).then_inc(once["log_0"], 1)
                        else:
                            total = by_chunk(sums[:])[:, :, L - 1:L]
                            nc.vector.tensor_scalar(prep[:, :, REC_AT["log1"]:REC_AT["log1"] + 1], total, -1.0, None,
                                                    ALU.mult).then_inc(once["log_first"], 1)
                            nc.vector.tensor_tensor(prep[:, :, REC_AT["log1"] + 1:REC_AT["log1"] + 1 + L],
                                                    by_chunk(sums[:]), total.broadcast_to([P, NT, L]),
                                                    ALU.subtract).then_inc(once["log_1"], 1)
                    for z in range(2):
                        a = th[2 + z]
                        read(f"a{z}")
                        nc.vector.tensor_scalar(a[:], a[:], 0.5, 0.5, ALU.mult, ALU.add).then_inc(once[f"a_{z}"], 1)
                        once_is(f"a_{z}")
                        nc.vector.tensor_scalar(th[z][:], a[:], table[:, par("k_a", i)], more[:, one_minus_ka(i)],
                                                ALU.mult, ALU.add).then_inc(once[f"kf_{z}"], 1)
                        once_is(f"kf_{z}")
                        nc.vector.tensor_tensor(out(f"kd{z}"), by_chunk(th[z][:]), by_chunk(kmix[:]),
                                                ALU.mult).then_inc(once[f"kd_{z}"], 1)
                    for z in range(2):
                        once_is(f"kd_{z}")
                    nc.vector.tensor_tensor(by_chunk(tmp[:]), out("kd0"), out("kd1"), ALU.add).then_inc(once["kd_both"], 1)
                    once_is("kd_both")
                    dve.wait_ge(filled[1], count(i - 1, TURNS.index("bonus"), 1))
                    nc.vector.scalar_tensor_tensor(by_chunk(rk[:]), by_chunk(tmp[:]), table[:, par("r_k", i)], out("r"),
                                                   ALU.mult, ALU.mult).then_inc(once["rk"], 1)
                    once_is("rk")
                    turn, s = slot("kk_sum")
                    dve.wait_ge(filled[s], count(i, turn, s))
                    nc.vector.tensor_scalar(banked(tmp[:]), cols(ps[s]), 1e-24, None, ALU.max).then_inc(emptied[s], 1)
                    once_is("kk_root")
                    nc.vector.reciprocal(tmp[:], tmp[:]).then_inc(once["kk_inverse"], 1)
                    once_is("kk_inverse")
                    nc.vector.tensor_tensor(out("kk"), by_chunk(kk[:]), by_chunk(tmp[:]), ALU.mult).then_inc(once["kk_done"], 1)
                    once_is("kk_done")
                    for z in range(2):
                        nc.vector.scalar_tensor_tensor(out(f"nb{z}"), out("kk"), -1.0, by_chunk(th[2 + z][:]), ALU.mult,
                                                       ALU.mult).then_inc(once[f"b_{z}"], 1)
                    read("bonus")
                    once_is("mixed_v")
                    nc.vector.tensor_tensor(by_chunk(bv[:]), by_chunk(bv[:]), out("v"), ALU.mult).then_inc(once["bonus_done"], 1)

KB = [(b * P, min(P, T - b * P)) for b in range(-(-T // P))]
NBLK = len(KB)
NQ = SEQ // P
QB = [META + b * P for b in range(NQ)]
SCORES = [(c, min(512, T - c)) for c in range(0, T, 512)]
LAMBDA_INIT = 0.8 - 0.6
GROUPS = [(0, 4), (4, 8), (8, 9)]
NG = len(GROUPS)


def learned_lambda(nc, sems, lq1, lk1, lq2, lk2, nlam):
    with ExitStack() as ctx:
        sb = lambda n, s: ctx.enter_context(nc.sbuf_tensor(n, s, F32))
        sem = lambda n: sems.enter_context(nc.semaphore(n))
        v = sb("ll_v", [P, 4, DQ])
        pr = sb("ll_pr", [P, 2, DQ])
        e = sb("ll_e", [P, 2])
        here, multiplied, summed, raised, less, done = (sem(f"ll_{n}") for n in (
            "here", "multiplied", "summed", "raised", "less", "done"))
        with nc.Block() as block:
            @block.sync
            def _(sp):
                for j, x in enumerate((lq1, lk1, lq2, lk2)):
                    sp.dma_start(v[:, j, :], x.broadcast_to([P, DQ])).then_inc(here, 16)

            @block.vector
            def _(dve):
                dve.wait_ge(here, 64)
                pairs = v[:].rearrange("p (m two) d -> p m two d", two=2)
                nc.vector.tensor_tensor(pr[:], pairs[:, :, 0, :], pairs[:, :, 1, :], ALU.mult).then_inc(multiplied, 1)
                dve.wait_ge(multiplied, 1)
                nc.vector.tensor_reduce(e[:], pr[:], AX, ALU.add).then_inc(summed, 1)
                dve.wait_ge(raised, 1)
                nc.vector.tensor_tensor(nlam[:], e[:, 1:2], e[:, 0:1], ALU.subtract).then_inc(less, 1)
                dve.wait_ge(less, 1)
                nc.vector.tensor_scalar(nlam[:], nlam[:], -LAMBDA_INIT, None, ALU.add).then_inc(done, 1)
                dve.wait_ge(done, 1)

            @block.scalar
            def _(act):
                act.wait_ge(summed, 1)
                nc.scalar.activation(e[:], e[:], ACT.Exp).then_inc(raised, 1)


def attention(nc, sems, kept_d, cos_d, sin_d, ident, nlam, att_d):
    SCALE = DQ ** -0.5
    with ExitStack() as ctx:
        sb = lambda n, s: ctx.enter_context(nc.sbuf_tensor(n, s, F32))
        sem = lambda n: sems.enter_context(nc.semaphore(n))
        cos, sin = sb("at_cos", [P, T]), sb("at_sin", [P, T])
        raw = {x: sb(f"at_{x}", [P, T]) for x in ("q", "q_half", "k", "k_half")}
        vT = sb("at_vT", [P, T])
        part = sb("at_part", [P, T])
        part2 = sb("at_part2", [P, T])
        qR = [sb(f"at_qR{s}", [P, T]) for s in range(2)]
        kR = [sb(f"at_kR{s}", [P, T]) for s in range(2)]
        v = [sb(f"at_v{s}", [P, NBLK, P]) for s in range(2)]
        pr = [[sb(f"at_p{m}{s}", [P, T]) for m in range(2)] for s in range(2)]
        pT = [sb(f"at_pT{s}", [P, NBLK, P]) for s in range(2)]
        mx = [sb(f"at_mx{s}", [P, 2]) for s in range(2)]
        nmx = [sb(f"at_nmx{s}", [P, 2]) for s in range(2)]
        sums = [sb(f"at_sums{s}", [P, 2]) for s in range(2)]
        inv = [sb(f"at_inv{s}", [P, 2]) for s in range(2)]
        coef = [sb(f"at_coef{s}", [P, 1]) for s in range(2)]
        o = [sb(f"at_o{s}", [P, P]) for s in range(2)]
        S = [ctx.enter_context(nc.psum_tensor(f"at_S{m}", [P, 3 * 512], F32)) for m in range(2)]
        tb = ctx.enter_context(nc.psum_tensor("at_tb", [P, 4, P], F32))
        ob = ctx.enter_context(nc.psum_tensor("at_ob", [P, 512], F32))

        tables_here, q_here, k_here, v_here = (sem(f"at_{n}_here") for n in ("tables", "q", "k", "v"))
        roped = sem("at_roped")
        v_turned, v_kept = sem("at_v_turned"), sem("at_v_kept")
        scored = [sem(f"at_scored{m}") for m in range(2)]
        maxed = [sem(f"at_maxed{m}") for m in range(2)]
        negated = [sem(f"at_negated{m}") for m in range(2)]
        raised = [sem(f"at_raised{m}") for m in range(2)]
        inverted, weighed, combined = sem("at_inverted"), sem("at_weighed"), sem("at_combined")
        turned, copied = sem("at_turned"), sem("at_copied")
        valued, o_scaled = sem("at_valued"), sem("at_o_scaled")
        o_stored = [sem(f"at_o_stored{s}") for s in range(2)]
        STEPS = 2 * NQ
        done = lambda g: g + STEPS + 1
        group_done = lambda g, j: NG * g + 2 * NG + j + 1

        with nc.Block() as block:
            @block.sync
            def _(sp):
                for sm in (*scored, *maxed, *raised, inverted, weighed, combined, valued, o_scaled):
                    sp.sem_inc(sm, STEPS)
                for sm in (turned, copied):
                    sp.sem_inc(sm, 2 * NG)
                for sm in (v_turned, v_kept):
                    sp.sem_inc(sm, 1)
                sp.sem_inc(roped, 6)
                for s in range(2):
                    sp.sem_inc(o_stored[s], 16)
                sp.dma_start(cos[:], cos_d).then_inc(tables_here, 16)
                sp.dma_start(sin[:], sin_d).then_inc(tables_here, 16)
                half = DQ // 2
                with sp.Fori(0, HEADS) as h:
                    for n, (x, name) in enumerate((("q", "att_q"), ("k", "att_k"))):
                        src = kept_d[KEPT.index(name), h]
                        here = (q_here, k_here)[n]
                        sp.wait_ge(roped, 6 * h + 3 * (n + 1))
                        sp.dma_start(raw[x][:], src).then_inc(here, 16)
                        for quarter in range(4):
                            other = quarter ^ 1
                            sp.dma_start(raw[x + "_half"][quarter * half:(quarter + 1) * half, :],
                                         src[other * half:(other + 1) * half, :]).then_inc(here, 16)
                    sp.wait_ge(v_turned, h + 1)
                    sp.dma_start(vT[:], kept_d[KEPT.index("att_v"), h]).then_inc(v_here, 16)

            @block.gpsimd
            def _(pool):
                pool.wait_ge(tables_here, 32)
                with pool.Fori(0, HEADS // 2) as i:
                    for s in range(2):
                        h = 2 * i + s
                        for n, (x, out) in enumerate((("q", qR[s]), ("k", kR[s]))):
                            pool.wait_ge((q_here, k_here)[n], 80 * h + 80)
                            pool.wait_ge(scored[1], done(NQ * h - NQ - 1))
                            at = 6 * h + 3 * n + 6
                            nc.gpsimd.tensor_tensor(part[:], raw[x][:], cos[:], ALU.mult).then_inc(roped, 1)
                            nc.gpsimd.tensor_tensor(part2[:], raw[x + "_half"][:], sin[:], ALU.mult).then_inc(roped, 1)
                            pool.wait_ge(roped, at + 2)
                            nc.gpsimd.tensor_tensor(out[:], part[:], part2[:], ALU.add).then_inc(roped, 1)
                            pool.wait_ge(roped, at + 3)

            @block.tensor
            def _(pe):
                with pe.Fori(0, HEADS // 2) as i:
                    for s in range(2):
                        h = 2 * i + s

                        def step(t):
                            return STEPS * i + NQ * s + t

                        def scores(t, m, parts=SCORES):
                            q0 = QB[t]
                            pe.wait_ge(raised[m], done(step(t) - 1))
                            rows = slice(DQ * m, DQ * m + DQ)
                            for c, w in parts:
                                ins = nc.tensor.matmul(S[m][:, c:c + w], qR[s][rows, q0:q0 + P],
                                                       kR[s][rows, c:c + w], start=True, stop=True)
                            if parts[-1] == SCORES[-1]:
                                ins.then_inc(scored[m], 1)

                        def turn_values():
                            pe.wait_ge(v_here, 16 * h + 16)
                            pe.wait_ge(raised[1], done(step(0) - 1))
                            for b, (k0, mk) in enumerate(KB):
                                ins = nc.tensor.transpose(S[1][0:mk, b * P:(b + 1) * P], vT[:, k0:k0 + mk], ident[:])
                            ins.then_inc(v_turned, 1)

                        def turn(t, j):
                            q0 = QB[t]
                            if j == 0:
                                pe.wait_ge(combined, done(step(t)))
                            pe.wait_ge(copied, group_done(step(t), j) - 1)
                            for n, b in enumerate(range(*GROUPS[j])):
                                k0, mk = KB[b]
                                ins = nc.tensor.transpose(tb[0:mk, n, 0:P],
                                                          pr[t % 2][0][:, k0:k0 + mk], ident[:])
                            ins.then_inc(turned, 1)

                        def values(t, j):
                            q0 = QB[t]
                            par = t % 2
                            if j == 0:
                                pe.wait_ge(o_scaled, done(step(t) - 1))
                                if t == 0:
                                    pe.wait_ge(v_kept, h + 2)
                            pe.wait_ge(copied, group_done(step(t), j))
                            for b in range(*GROUPS[j]):
                                mk = KB[b][1]
                                ins = nc.tensor.matmul(ob[:, 0:P], pT[par][0:mk, b, 0:P], v[s][0:mk, b, :],
                                                       start=(b == 0), stop=(b == NBLK - 1))
                            if j == NG - 1:
                                ins.then_inc(valued, 1)

                        for t in range(NQ + 1):
                            if t == 0:
                                pe.wait_ge(roped, 6 * h + 12)
                            if t < NQ:
                                scores(t, 0)
                            if t == 0:
                                turn_values()
                                pe.wait_ge(v_kept, h + 2)
                            if t > 0:
                                turn(t - 1, 0)
                            if t < NQ:
                                scores(t, 1, SCORES[:1])
                            if t > 0:
                                turn(t - 1, 1)
                                values(t - 1, 0)
                            if t < NQ:
                                scores(t, 1, SCORES[1:])
                            if t > 0:
                                turn(t - 1, 2)
                                values(t - 1, 1)
                                values(t - 1, 2)

            @block.scalar
            def _(act):
                with act.Fori(0, HEADS // 2) as i:
                    for s in range(2):
                        def step(t):
                            return STEPS * i + NQ * s + t

                        def keep_turned(t, j):
                            q0 = QB[t]
                            par = t % 2
                            if j == 0:
                                act.wait_ge(valued, done(step(t) - 2))
                            act.wait_ge(turned, group_done(step(t), j))
                            b0, b1 = GROUPS[j]
                            mk = KB[b0][1]
                            nc.scalar.copy(pT[par][0:mk, b0:b1, 0:P], tb[0:mk, 0:b1 - b0, 0:P]).then_inc(copied, 1)

                        def raise_scores(t, m):
                            par = t % 2
                            if m == 0:
                                act.wait_ge(turned, group_done(step(t) - 2, NG - 1))
                                act.wait_ge(combined, done(step(t) - 2))
                            act.wait_ge(negated[m], step(t) + 1)
                            nc.scalar.activation(pr[par][m][:], S[m][:, 0:T], ACT.Exp,
                                                 bias=nmx[par][:, m:m + 1], scale=SCALE,
                                                 accum_out=sums[par][:, m:m + 1]).then_inc(raised[m], 1)

                        for t in range(NQ + 1):
                            if t > 0:
                                keep_turned(t - 1, 0)
                            if t < NQ:
                                raise_scores(t, 0)
                            if t == 0:
                                act.wait_ge(v_turned, 2 * i + s + 2)
                                nc.scalar.copy(v[s][:, 0:NBLK - 1, :].rearrange("p b d -> p (b d)"),
                                               S[1][:, 0:(NBLK - 1) * P])
                                nc.scalar.copy(v[s][0:KB[-1][1], NBLK - 1, :],
                                               S[1][0:KB[-1][1], (NBLK - 1) * P:NBLK * P]).then_inc(v_kept, 1)
                            if t > 0:
                                for j in range(1, NG):
                                    keep_turned(t - 1, j)
                            if t < NQ:
                                raise_scores(t, 1)
                            if t > 0:
                                q0 = QB[t - 1]
                                par = (t - 1) % 2
                                act.wait_ge(o_scaled, done(step(t - 1)))
                                act.dma_start(att_d[q0:q0 + P, bass.ts(2 * i + s, P)],
                                              o[par][:]).then_inc(o_stored[par], 16)
                for s in range(2):
                    act.wait_ge(o_stored[s], 16 * NQ * HEADS // 2 + 16)

            @block.vector
            def _(dve):
                with dve.Fori(0, HEADS // 2) as i:
                    for s in range(2):
                        def step(t):
                            return STEPS * i + NQ * s + t

                        for t in range(NQ + 1):
                            par = t % 2
                            if t < NQ:
                                for m in range(2):
                                    dve.wait_ge(scored[m], done(step(t)))
                                    dve.wait_ge(raised[m], done(step(t) - 2))
                                    nc.vector.tensor_reduce(mx[par][:, m:m + 1], S[m][:, 0:T], AX,
                                                            ALU.max).then_inc(maxed[m], 1)
                                    dve.wait_ge(maxed[m], done(step(t)))
                                    nc.vector.tensor_scalar(nmx[par][:, m:m + 1], mx[par][:, m:m + 1], -SCALE,
                                                            None, ALU.mult).then_inc(negated[m], 1)
                            if t > 0:
                                dve.wait_ge(valued, done(step(t - 1)))
                                dve.wait_ge(o_stored[par ^ 1], 8 * (step(t - 1) - (par ^ 1)) + 16)
                                nc.vector.tensor_scalar(o[par ^ 1][:], ob[:, 0:P],
                                                        inv[par ^ 1][:, 0:1], None, ALU.mult).then_inc(o_scaled, 1)
                            if t < NQ:
                                for m in range(2):
                                    dve.wait_ge(raised[m], done(step(t)))
                                nc.vector.reciprocal(inv[par][:], sums[par][:]).then_inc(inverted, 1)
                                dve.wait_ge(inverted, done(step(t)))
                                nc.vector.scalar_tensor_tensor(coef[par][:], inv[par][:, 1:2], nlam[:],
                                                               sums[par][:, 0:1], ALU.mult,
                                                               ALU.mult).then_inc(weighed, 1)
                                dve.wait_ge(weighed, done(step(t)))
                                nc.vector.scalar_tensor_tensor(pr[par][0][:], pr[par][1][:],
                                                               coef[par][:], pr[par][0][:], ALU.mult,
                                                               ALU.add).then_inc(combined, 1)

UNITS = 4
LEVELS = [2 ** n for n in range(1, 7)]
NLEV = len(LEVELS)
PAIRS = NT // 2
SLOTS = 5


def recurrence_masks():
    row, col = np.arange(L)[:, None], np.arange(L)[None, :]
    later = [col > row, col < row]
    m_turned = np.stack([np.stack([f, f | (row == col)]) for f in later], 0)
    m_plain = np.stack([f.T for f in later], 0)
    def join(size):
        return (row // (2 * size) == col // (2 * size)) & (row // size != col // size)
    first = np.stack([m_plain & join(1), m_turned[:, 0] & join(1)], 0)
    levels = np.stack([m_turned[:, 0] & join(size) for size in LEVELS], 0)
    parts = [m_turned.reshape(4, L, L), first.reshape(4, L, L), levels.reshape(2 * NLEV, L, L), (row == col)[None]]
    return np.concatenate(parts, 0).transpose(1, 0, 2).astype(np.float32).copy()


M_TURNED, M_FIRST, M_LEVEL, M_EYE = 0, 4, 8, 8 + 2 * NLEV
NMASK = M_EYE + 1


def pieces():
    out = [("raise", 0), ("raise", 1), ("front", 0), ("front", 1)]
    for p in range(PAIRS):
        a, b = 2 * p, 2 * p + 1
        chain = [(part, k) for k in (a - 2, b - 2) for part in ("chain_w", "chain_u", "chain_s")] if p else []
        ahead = {0: ("raise", a + 2), 2: ("front", a + 2), 3: ("raise", b + 2), 4: ("front", b + 2)} if p < PAIRS - 1 else {}
        for lev in range(NLEV):
            out += [("turn", a, lev), ("turn", b, lev)]
            out += chain[lev:lev + 1]
            out += [ahead[lev]] if lev in ahead else []
            out += [("join", a, lev), ("join", b, lev)]
    return out + [(part, k) for k in (NT - 2, NT - 1) for part in ("chain_w", "chain_u", "chain_s")]


PIECES = pieces()
SMALL = []
for _piece in PIECES:
    if _piece[0] == "front":
        SMALL += [(name, _piece[1]) for name in ("rows_kb", "rows_v", "mb0", "mb1", "mk0", "mk1", "m")]
    elif _piece[0] == "chain_s":
        SMALL += [("s", _piece[1]), ("y", _piece[1])]
    elif _piece[0] in ("chain_w", "chain_u"):
        SMALL += [(_piece[0][-1], _piece[1])]
assert len(SMALL) % 2 == 0
NSMALL = len(SMALL) // 2


def recurrence(nc, sems, prep_d, masks_d, ident, y_d):
    with ExitStack() as ctx:
        sb = lambda n, s: ctx.enter_context(nc.sbuf_tensor(n, s, F32))
        sem = lambda n: sems.enter_context(nc.semaphore(n))
        both = lambda name, shape: [[sb(f"rc_{name}{s}{z}", shape) for z in range(2)] for s in range(SLOTS)]
        each = lambda name, shape: [sb(f"rc_{name}{s}", shape) for s in range(SLOTS)]
        masks = sb("rc_masks", [L, NMASK, L])
        rec = both("rec", [P, HALF_REC])
        grow = both("grow", [P, 2, L + 1])
        g_end = both("g_end", [P, 1])
        shrink = both("shrink", [P, L])
        ar = both("ar", [P, 2, 2, L])
        kb = both("kb", [P, 2, L])
        rows = each("rows", [L, 6, P])
        mb = each("mb", [L, 2, 2, 2, L])
        mk = each("mk", [L, 2, 2, 2, L])
        m = each("m", [L, UNITS, L])
        x = each("x", [L, UNITS, L])
        xT = each("xT", [L, UNITS, L])
        wT = each("wT", [L, UNITS, L])
        state = [sb(f"rc_state{s}", [P, 2, P]) for s in range(2)]
        decayed = sb("rc_decayed", [P, 2, P])
        w = sb("rc_w", [L, UNITS, N])
        u = sb("rc_u", [L, UNITS, N])
        y = [sb(f"rc_y{s}", [L, UNITS, N]) for s in range(2)]
        bank = [ctx.enter_context(nc.psum_tensor(f"rc_bank{b}", [P, 512], F32)) for b in range(8)]

        masks_here, zeroed = sem("rc_masks_here"), sem("rc_zeroed")
        rec_here = [sem(f"rc_rec_here{s}") for s in range(SLOTS)]
        raised, spread, decayed_done, x_first = (sem(f"rc_{n}") for n in ("raised", "spread", "decayed", "x_first"))
        state_cleared = sem("rc_state_cleared")
        y_stored = [sem(f"rc_y_stored{s}") for s in range(2)]
        turned = [sem(f"rc_turned{g}") for g in range(2)]
        wT_done = [sem(f"rc_wT_done{g}") for g in range(2)]
        joinedT = [sem(f"rc_joinedT{g}") for g in range(2)]
        xT_done = [sem(f"rc_xT_done{g}") for g in range(2)]
        back = [sem(f"rc_back{g}") for g in range(2)]
        x_done = [sem(f"rc_x_done{g}") for g in range(2)]
        filled = [sem(f"rc_filled{b}") for b in range(2)]
        emptied = [sem(f"rc_emptied{b}") for b in range(2)]

        LC = NLEV * PAIRS
        XC = (NLEV - 1) * PAIRS

        def step(i, k):
            return NT * i + k + 1 + NT

        def level(i, k, lev):
            return LC * i + NLEV * (k // 2) + lev + 1 + LC

        def x_level(i, k, lev):
            return XC * i + (NLEV - 1) * (k // 2) + lev + 1 + XC

        def small(i, name, k):
            n = SMALL.index((name, k % NT))
            return n % 2, NSMALL * (i + k // NT) + n // 2 + 1 + NSMALL

        def wait_filled(eng, i, name, k):
            b, n = small(i, name, k)
            eng.wait_ge(filled[b], n)
            return bank[6 + b]

        def wait_emptied(eng, i, name, k):
            b, n = small(i, name, k)
            eng.wait_ge(emptied[b], n)

        def units(ap, width):
            return ap[:, 0:UNITS * width].rearrange("p (u w) -> p u w", u=UNITS)

        def by_direction(ap):
            return ap.rearrange("p (z h) w -> p z h w", z=2)

        def per_head(at):
            return masks[:, at:at + 2, :].unsqueeze(2).broadcast_to([L, 2, 2, L])

        def part(z, name):
            return REC_AT[name if name in REC_AT else name + str(z)] - (z * (REC - HALF_REC))

        head = [slice(N * h, N * h + N) for h in range(2)]
        at_pos = [slice(1, L + 1), slice(0, L)]
        before_pos = [slice(0, L), slice(1, L + 1)]

        with nc.Block() as block:
            @block.sync
            def _(sp):
                for sm in (raised, spread, decayed_done):
                    sp.sem_inc(sm, NT)
                sp.sem_inc(x_first, 4 * NT)
                for g in range(2):
                    sp.sem_inc(y_stored[g], 32)
                    for sm in (turned[g], wT_done[g], joinedT[g], xT_done[g]):
                        sp.sem_inc(sm, LC)
                    for sm in (back[g], x_done[g]):
                        sp.sem_inc(sm, XC)
                    for sm in (filled[g], emptied[g]):
                        sp.sem_inc(sm, NSMALL)
                sp.dma_start(masks[:], masks_d).then_inc(masks_here, 16)
                with sp.Fori(0, HEADS) as i:
                    for k in range(NT):
                        s = k % SLOTS
                        wait_filled(sp, i, "rows_v", k - SLOTS)
                        sp.dma_start(rec[s][0][:], prep_d[i, k, :, 0:HALF_REC]).then_inc(rec_here[s], 16)
                        sp.dma_start(rec[s][1][:], prep_d[i, NT - 1 - k, :, REC - HALF_REC:REC]).then_inc(rec_here[s], 16)

            @block.gpsimd
            def _(pool):
                n = 0
                pool.wait_ge(masks_here, 16)
                pool.wait_ge(zeroed, 4 * SLOTS)
                with pool.Fori(0, HEADS) as i:
                    for piece, k, *_ in PIECES:
                        s = k % SLOTS
                        if piece == "raise":
                            pool.wait_ge(raised, step(i, k))
                            wait_filled(pool, i, "y", k - SLOTS)
                            for z in range(2):
                                src, g = rec[s][z], grow[s][z]
                                for n, (x_name, at) in enumerate((("kk", before_pos[z]), ("r", at_pos[z]))):
                                    o = part(z, x_name)
                                    nc.gpsimd.tensor_tensor(ar[s][z][:, :, n, :],
                                                            src[:, o:o + L].unsqueeze(1).broadcast_to([P, 2, L]),
                                                            g[:, :, at], ALU.mult)
                                o = part(z, "kd")
                                last = nc.gpsimd.tensor_tensor(
                                    kb[s][z][:], src[:, o:o + 2 * L].rearrange("p (a t) -> p a t", a=2),
                                    shrink[s][z][:].unsqueeze(1).broadcast_to([P, 2, L]), ALU.mult)
                            last.then_inc(spread, 1)
                        elif piece == "front":
                            base = 4 * (step(i, k) - 1)
                            wait_emptied(pool, i, "u", k - SLOTS)
                            wait_emptied(pool, i, "m", k)
                            nc.gpsimd.tensor_tensor(by_direction(x[s][:]), by_direction(m[s][:]), per_head(M_FIRST),
                                                    ALU.mult).then_inc(x_first, 1)
                            nc.gpsimd.tensor_tensor(by_direction(xT[s][:]), mb[s][:, :, :, 0, :], per_head(M_FIRST + 2),
                                                    ALU.mult).then_inc(x_first, 1)
                            for n, dst in enumerate((x, xT)):
                                pool.wait_ge(x_first, base + n + 1)
                                nc.gpsimd.tensor_tensor(dst[s][:], dst[s][:],
                                                        masks[:, M_EYE:M_EYE + 1, :].broadcast_to([L, UNITS, L]),
                                                        ALU.add).then_inc(x_first, 1)

            @block.tensor
            def _(pe):
                pe.wait_ge(masks_here, 16)
                with pe.Fori(0, HEADS) as i:
                    def take(name, k):
                        b, n = small(i, name, k)
                        pe.wait_ge(emptied[b], n - 1)
                        return bank[6 + b], filled[b]

                    for piece, k, *lev in PIECES:
                        s, g = k % SLOTS, k % 2
                        if piece == "front":
                            pe.wait_ge(spread, step(i, k))
                            out, done = take("rows_kb", k)
                            for j in range(4):
                                ins = nc.tensor.transpose(out[0:L, j * P:(j + 1) * P], kb[s][j % 2][:, 1 - j // 2, :], ident[:])
                            ins.then_inc(done, 1)
                            out, done = take("rows_v", k)
                            for z in range(2):
                                o = part(z, "v")
                                ins = nc.tensor.transpose(out[0:L, z * P:(z + 1) * P], rec[s][z][:, o:o + L], ident[:])
                            ins.then_inc(done, 1)
                            for n, name in ((1, "mb"), (0, "mk")):
                                for z in range(2):
                                    out, done = take(f"{name}{z}", k)
                                    nc.tensor.matmul(out[0:L, 0:4 * L], kb[s][z][:, n, :],
                                                     ar[s][z][:].rearrange("p h a t -> p (h a t)"),
                                                     start=True, stop=True).then_inc(done, 1)
                            out, done = take("m", k)
                            for z in range(2):
                                wait_emptied(pe, i, f"mb{z}", k)
                                for h in range(2):
                                    ins = nc.tensor.transpose(units(out[0:L, :], L)[:, 2 * z + h, :],
                                                              mb[s][:, z, h, 0, :], ident[0:L, 0:L])
                            ins.then_inc(done, 1)
                        elif piece == "turn":
                            lev, = lev
                            if lev == 0:
                                pe.wait_ge(x_first, 4 * step(i, k))
                            pe.wait_ge(xT_done[g], level(i, k, lev - 1))
                            for j in range(UNITS):
                                ins = nc.tensor.matmul(units(bank[3 * g][0:L, :], L)[:, j, :], m[s][:, j, :], xT[s][:, j, :],
                                                       start=True, stop=True)
                            ins.then_inc(turned[g], 1)
                            if lev > 0:
                                for j in range(UNITS):
                                    ins = nc.tensor.transpose(units(bank[3 * g + 2][0:L, :], L)[:, j, :], xT[s][:, j, :],
                                                              ident[0:L, 0:L])
                                ins.then_inc(back[g], 1)
                        elif piece == "join":
                            lev, = lev
                            pe.wait_ge(wT_done[g], level(i, k, lev))
                            pe.wait_ge(x_done[g], x_level(i, k, lev - 1))
                            for j in range(UNITS):
                                ins = nc.tensor.matmul(units(bank[3 * g + 1][0:L, :], L)[:, j, :], x[s][:, j, :], wT[s][:, j, :],
                                                       start=True, stop=True)
                            ins.then_inc(joinedT[g], 1)
                        elif piece == "chain_w":
                            if k == 0:
                                pe.wait_ge(state_cleared, i + 1)
                            else:
                                wait_emptied(pe, i, "s", k - 1)
                            out, done = take("w", k)
                            for j in range(UNITS):
                                z, h = divmod(j, 2)
                                o = units(out[0:L, :], N)[:, j, :]
                                nc.tensor.matmul(o, ar[s][z][:, h, 0, :], state[g][:, z, head[h]], start=True, stop=False)
                                ins = nc.tensor.matmul(o, mk[s][:, z, h, 0, :], rows[s][:, 4 + z, head[h]],
                                                       start=False, stop=True)
                            ins.then_inc(done, 1)
                        elif piece == "chain_u":
                            wait_emptied(pe, i, "w", k)
                            pe.wait_ge(xT_done[g], level(i, k, NLEV - 1))
                            out, done = take("u", k)
                            for j in range(UNITS):
                                ins = nc.tensor.matmul(units(out[0:L, :], N)[:, j, :], xT[s][:, j, :], w[:, j, :],
                                                       start=True, stop=True)
                            ins.then_inc(done, 1)
                        elif piece == "chain_s":
                            wait_emptied(pe, i, "u", k)
                            out, done = take("s", k)
                            for z in range(2):
                                o = out[:, z * P:(z + 1) * P]
                                nc.tensor.matmul(o, rows[s][:, z, :], u[:, 2 * z:2 * z + 2, :].rearrange("p h v -> p (h v)"),
                                                 start=True, stop=False)
                                ins = nc.tensor.matmul(o, rows[s][:, 2 + z, :], rows[s][:, 4 + z, :], start=False, stop=True)
                            ins.then_inc(done, 1)
                            out, done = take("y", k)
                            for j in range(UNITS):
                                z, h = divmod(j, 2)
                                o = units(out[0:L, :], N)[:, j, :]
                                nc.tensor.matmul(o, ar[s][z][:, h, 1, :], state[g][:, z, head[h]], start=True, stop=False)
                                nc.tensor.matmul(o, mb[s][:, z, h, 1, :], u[:, j, :], start=False, stop=False)
                                ins = nc.tensor.matmul(o, mk[s][:, z, h, 1, :], rows[s][:, 4 + z, head[h]],
                                                       start=False, stop=True)
                            ins.then_inc(done, 1)

            @block.scalar
            def _(act):
                with act.Fori(0, HEADS) as i:
                    for piece, k, *lev in PIECES:
                        s, g = k % SLOTS, k % 2
                        if piece == "raise":
                            act.wait_ge(rec_here[s], 64 * i + 32 * (k // SLOTS) + 32)
                            act.wait_ge(spread, step(i, k - SLOTS))
                            wait_emptied(act, i, "s", k - SLOTS)
                            for z in range(2):
                                o = part(z, "log")
                                sign = (1.0, -1.0)[z]
                                for h in range(2):
                                    nc.scalar.activation(grow[s][z][head[h], h, :], rec[s][z][head[h], o:o + L + 1],
                                                         ACT.Exp, scale=sign)
                                at_end = o + (L, 0)[z]
                                nc.scalar.activation(g_end[s][z][:], rec[s][z][:, at_end:at_end + 1], ACT.Exp, scale=sign)
                                first = o + (1, 0)[z]
                                last = nc.scalar.activation(shrink[s][z][:], rec[s][z][:, first:first + L], ACT.Exp,
                                                            scale=-sign)
                            last.then_inc(raised, 1)
                        elif piece == "front":
                            wait_filled(act, i, "y", k - SLOTS)
                            for name, j0, j1 in (("rows_kb", 0, 4), ("rows_v", 4, 6)):
                                b, _n = small(i, name, k)
                                src = wait_filled(act, i, name, k)
                                nc.scalar.copy(rows[s][:, j0:j1, :].rearrange("p j c -> p (j c)"),
                                               src[0:L, 0:(j1 - j0) * P]).then_inc(emptied[b], 1)
                            b, _n = small(i, "m", k)
                            src = wait_filled(act, i, "m", k)
                            nc.scalar.copy(m[s][:], units(src[0:L, :], L)).then_inc(emptied[b], 1)
                        elif piece == "turn" and lev[0] > 0:
                            act.wait_ge(back[g], x_level(i, k, lev[0] - 1))
                            nc.scalar.copy(x[s][:], units(bank[3 * g + 2][0:L, :], L)).then_inc(x_done[g], 1)
                        elif piece == "chain_w":
                            if k == 0:
                                act.wait_ge(state_cleared, i + 1)
                            else:
                                wait_emptied(act, i, "s", k - 1)
                            for z in range(2):
                                ins = nc.scalar.activation(decayed[:, z, :], state[g][:, z, :], ACT.Copy,
                                                           scale=g_end[s][z][:])
                            ins.then_inc(decayed_done, 1)
                        if piece in ("chain_w", "chain_u"):
                            name, dst = ("w", w) if piece == "chain_w" else ("u", u)
                            b, _n = small(i, name, k)
                            src = wait_filled(act, i, name, k)
                            nc.scalar.copy(dst[:], units(src[0:L, :], N)).then_inc(emptied[b], 1)
                        elif piece == "chain_s":
                            act.wait_ge(y_stored[g], 32 * PAIRS * i + 32 * (k // 2) + 32)
                            b, _n = small(i, "y", k)
                            src = wait_filled(act, i, "y", k)
                            nc.scalar.copy(y[g][:], units(src[0:L, :], N)).then_inc(emptied[b], 1)
                            wait_emptied(act, i, "y", k)
                            for z, c in enumerate((k, NT - 1 - k)):
                                act.dma_start(y_d[z, c * L:(c + 1) * L, bass.ts(i, P)],
                                              y[g][:, 2 * z:2 * z + 2, :].rearrange("p h v -> p (h v)")) \
                                    .then_inc(y_stored[g], 16)
                for g in range(2):
                    act.wait_ge(y_stored[g], 32 * PAIRS * HEADS + 32)

            @block.vector
            def _(dve):
                for s in range(SLOTS):
                    for z in range(2):
                        for h in range(2):
                            nc.vector.memset(grow[s][z][head[1 - h], h, :], 0.0).then_inc(zeroed, 1)
                dve.wait_ge(masks_here, 16)
                with dve.Fori(0, HEADS) as i:
                    wait_filled(dve, i, "y", -1)
                    wait_emptied(dve, i, "s", -1)
                    nc.vector.memset(state[0][:], 0.0).then_inc(state_cleared, 1)
                    for piece, k, *lev in PIECES:
                        s, g = k % SLOTS, k % 2
                        if piece == "front":
                            wait_filled(dve, i, "y", k - SLOTS)
                            for name, dst in (("mb", mb), ("mk", mk)):
                                for z in range(2):
                                    b, _n = small(i, f"{name}{z}", k)
                                    src = wait_filled(dve, i, f"{name}{z}", k)
                                    at = M_TURNED + 2 * z
                                    nc.vector.tensor_tensor(
                                        dst[s][:, z, :, :, :], src[0:L, 0:4 * L].rearrange("p (h a t) -> p h a t", h=2, a=2),
                                        masks[:, at:at + 2, :].unsqueeze(1).broadcast_to([L, 2, 2, L]),
                                        ALU.mult).then_inc(emptied[b], 1)
                        elif piece == "turn":
                            lev, = lev
                            dve.wait_ge(turned[g], level(i, k, lev))
                            nc.vector.tensor_tensor(by_direction(wT[s][:]), by_direction(units(bank[3 * g][0:L, :], L)),
                                                    per_head(M_LEVEL + 2 * lev), ALU.mult).then_inc(wT_done[g], 1)
                        elif piece == "join":
                            lev, = lev
                            dve.wait_ge(joinedT[g], level(i, k, lev))
                            nc.vector.tensor_tensor(xT[s][:], units(bank[3 * g + 1][0:L, :], L), xT[s][:],
                                                    ALU.add).then_inc(xT_done[g], 1)
                        elif piece == "chain_s":
                            b, _n = small(i, "s", k)
                            src = wait_filled(dve, i, "s", k)
                            dve.wait_ge(decayed_done, step(i, k))
                            for z in range(2):
                                ins = nc.vector.scalar_tensor_tensor(state[1 - g][:, z, :], src[:, z * P:(z + 1) * P],
                                                                     g_end[s][z][:], decayed[:, z, :], ALU.mult,
                                                                     ALU.add)
                            ins.then_inc(emptied[b], 1)

DOWN_EARLY = 12
TOK = SEQ // P
SUBLN_EPS = 1e-5
LNX_EPS = 64e-5


def merge_and_mix(nc, sems, x, att_d, y_d, kept_d, w_out, post_g, ident, table, u2T, h2_d):
    with ExitStack() as ctx:
        sb = lambda n, s: ctx.enter_context(nc.sbuf_tensor(n, s, F32))
        sem = lambda n: sems.enter_context(nc.semaphore(n))
        two = lambda n, s: [sb(f"mm_{n}{p}", s) for p in range(2)]
        wo = sb("mm_wo", [P, KC, D])
        gain = sb("mm_gain", [P, D])
        sub = sb("mm_sub", [P, 1])
        eps = sb("mm_eps", [P, 3])
        att, yf, yb, h = two("att", [P, D]), two("yf", [P, D]), two("yb", [P, D]), two("h", [P, D])
        sq = sb("mm_sq", [P, D])
        sq_y = sb("mm_sq_y", [P, D])
        sq_m = sb("mm_sq_m", [P, D])
        a_st, y_st, m_st = two("a_st", [P, 3, 8]), two("y_st", [P, 4, 16]), two("m_st", [P, 6])
        names = ("g", "bonus_v", "gate_a", "gate_r")
        fm = {n: two(n, [P, KC, P]) for n in names}
        ma, mr, mT = sb("mm_ma", [P, KC, P]), sb("mm_mr", [P, KC, P]), two("mT", [P, KC, P])
        h2, un = two("h2", [P, D]), two("un", [P, D])
        ps = [ctx.enter_context(nc.psum_tensor(f"mm_ps{j}", [P, D], F32)) for j in range(4)]
        ps_a, ps_y, ps_m, ps_u = ps

        consts, const_done = sem("mm_consts"), sem("mm_const_done")
        tok_here = [sem(f"mm_tok_here{p}") for p in range(2)]
        fm_here = [sem(f"mm_fm_here{p}") for p in range(2)]
        x_here = [sem(f"mm_x_here{p}") for p in range(2)]
        h2_stored = [sem(f"mm_h2_stored{p}") for p in range(2)]
        st = {n: sem(f"mm_{n}") for n in (
            "a_squared", "a_summed", "a_rooted", "a_inverse", "a_normed", "a_turned",
            "y_added", "y_summed", "y_mean", "y_centred", "y_squared", "y_varied", "y_rooted", "y_inverse", "y_normed",
            "y_turned", "bonus_shifted", "gated", "ma", "mr_scaled", "mr_shifted", "mr", "merged", "projected",
            "m_squared", "m_rooted", "m_inverse", "m_normed", "h2", "h_squared", "h_rooted", "h_inverse", "u_normed",
            "u_turned", "u_kept")}

        def wait(eng, name, t):
            if t >= 0:
                eng.wait_ge(st[name], t + 1)

        def heads(ap, n):
            return ap.rearrange("p (h c) -> p h c", h=n)

        def columns(name):
            at = PAR[name][0]
            return table[:, at:at + KC].unsqueeze(2).broadcast_to([P, KC, P])

        def tiles(ap):
            return ap.rearrange("p (k t) -> p k t", k=KC)

        STAGES = [(s, t) for step in range(TOK + 4)
                  for s, t in (("project", step - 2), ("merge", step - 1), ("mix", step - 3), ("heads", step),
                               ("norm", step - 3), ("turn", step - 4))
                  if 0 <= t < TOK]

        with nc.Block() as block:
            @block.sync
            def _(sp):
                def load_tokens(t):
                    p = t % 2
                    rows = slice(META + t * P, META + (t + 1) * P)
                    wait(sp, "a_turned", t - 2)
                    wait(sp, "y_turned", t - 2)
                    sp.dma_start(att[p][:], att_d[rows, :]).then_inc(tok_here[p], 16)
                    sp.dma_start(yf[p][:], y_d[0, rows, :]).then_inc(tok_here[p], 16)
                    sp.dma_start(yb[p][:], y_d[1, rows, :]).then_inc(tok_here[p], 16)

                def load_features(t):
                    p = t % 2
                    wait(sp, "merged", t - 2)
                    for n in names:
                        src = kept_d[KEPT.index(n), :, :, META + t * P:META + (t + 1) * P]
                        sp.dma_start(fm[n][p][:], src.rearrange("k p t -> p k t")).then_inc(fm_here[p], 16)

                def load_x(t):
                    p = t % 2
                    wait(sp, "h2", t - 2)
                    sp.dma_start(h[p][:], x[t * P:(t + 1) * P, :]).then_inc(x_here[p], 16)

                load_tokens(0)
                sp.dma_start(gain[:], post_g.broadcast_to([P, D])).then_inc(consts, 16)
                sp.dma_start(wo[:], w_out).then_inc(consts, 16)
                load_features(0)
                for t in range(1, TOK):
                    load_tokens(t)
                    load_features(t)
                    load_x(t - 1)
                load_x(TOK - 1)

            @block.gpsimd
            def _(pool):
                for s, t in STAGES:
                    p = t % 2
                    if s == "heads":
                        pool.wait_ge(tok_here[p], 48 * (t // 2) + 48)
                        nc.gpsimd.tensor_tensor(yf[p][:], yf[p][:], yb[p][:], ALU.add).then_inc(st["y_added"], 1)
                    elif s == "merge":
                        pool.wait_ge(fm_here[p], 64 * (t // 2) + 64)
                        nc.gpsimd.tensor_tensor(fm["bonus_v"][p][:], fm["bonus_v"][p][:], columns("lnx_b"),
                                                ALU.add).then_inc(st["bonus_shifted"], 1)
                        nc.gpsimd.tensor_tensor(fm["g"][p][:], fm["g"][p][:], fm["gate_r"][p][:],
                                                ALU.mult).then_inc(st["gated"], 1)
                    elif s == "mix":
                        wait(pool, "m_normed", t)
                        pool.wait_ge(x_here[p], 16 * (t // 2) + 16)
                        wait(pool, "u_turned", t - 2)
                        if t >= 2:
                            pool.wait_ge(h2_stored[p], 16 * (t // 2))
                        nc.gpsimd.tensor_tensor(h2[p][:], h2[p][:], h[p][:], ALU.add).then_inc(st["h2"], 1)

            @block.tensor
            def _(pe):
                for s, t in STAGES:
                    p = t % 2
                    if s == "heads":
                        for name, src, dst, reader in (("a", att, ps_a, "ma"), ("y", yf, ps_y, "mr_scaled")):
                            wait(pe, f"{name}_normed", t)
                            wait(pe, reader, t - 1)
                            for k in range(KC):
                                ins = nc.tensor.transpose(dst[:, k * P:(k + 1) * P], src[p][:, k * P:(k + 1) * P], ident[:])
                            ins.then_inc(st[f"{name}_turned"], 1)
                    elif s == "project":
                        wait(pe, "merged", t)
                        wait(pe, "m_normed", t - 1)
                        if t == 0:
                            pe.wait_ge(consts, 32)
                        for n in range(2):
                            for k in range(KC):
                                ins = nc.tensor.matmul(ps_m[:, n * 512:(n + 1) * 512], mT[p][:, k, :],
                                                       wo[:, k, n * 512:(n + 1) * 512], start=(k == 0), stop=(k == KC - 1))
                        ins.then_inc(st["projected"], 1)
                    elif s == "turn":
                        wait(pe, "u_normed", t)
                        wait(pe, "u_kept", t - 1)
                        for k in range(KC):
                            ins = nc.tensor.transpose(ps_u[:, k * P:(k + 1) * P], un[p][:, k * P:(k + 1) * P], ident[:])
                        ins.then_inc(st["u_turned"], 1)

            @block.scalar
            def _(act):
                act.wait_ge(const_done, 4)
                for s, t in STAGES:
                    p = t % 2
                    if s == "heads":
                        act.wait_ge(tok_here[p], 48 * (t // 2) + 48)
                        wait(act, "a_summed", t - 1)
                        nc.scalar.activation(sq[:], att[p][:], ACT.Square).then_inc(st["a_squared"], 1)
                        wait(act, "a_summed", t)
                        nc.scalar.activation(a_st[p][:, 1, :], a_st[p][:, 0, :], ACT.Sqrt, bias=eps[:, 0:1],
                                             scale=1.0 / P).then_inc(st["a_rooted"], 1)
                        wait(act, "y_centred", t)
                        nc.scalar.activation(sq_y[:], yf[p][:], ACT.Square).then_inc(st["y_squared"], 1)
                        wait(act, "y_varied", t)
                        nc.scalar.activation(y_st[p][:, 2, :], y_st[p][:, 1, :], ACT.Sqrt, bias=eps[:, 1:2],
                                             scale=1.0 / N).then_inc(st["y_rooted"], 1)
                    elif s == "mix":
                        wait(act, "projected", t)
                        nc.scalar.activation(sq_m[:], ps_m[:], ACT.Square,
                                             accum_out=m_st[p][:, 0:1]).then_inc(st["m_squared"], 1)
                        wait(act, "m_squared", t)
                        nc.scalar.activation(m_st[p][:, 1:2], m_st[p][:, 0:1], ACT.Sqrt, bias=eps[:, 2:3],
                                             scale=1.0 / D).then_inc(st["m_rooted"], 1)
                    elif s == "norm":
                        wait(act, "h2", t)
                        act.dma_start(h2_d[t * P:(t + 1) * P, :], h2[p][:]).then_inc(h2_stored[p], 16)
                        nc.scalar.activation(sq_m[:], h2[p][:], ACT.Square,
                                             accum_out=m_st[p][:, 3:4]).then_inc(st["h_squared"], 1)
                        wait(act, "h_squared", t)
                        nc.scalar.activation(m_st[p][:, 4:5], m_st[p][:, 3:4], ACT.Sqrt, bias=eps[:, 2:3],
                                             scale=1.0 / D).then_inc(st["h_rooted"], 1)
                        wait(act, "h_inverse", t)
                        wait(act, "u_turned", t - 2)
                        nc.scalar.activation(un[p][:], h2[p][:], ACT.Copy,
                                             scale=m_st[p][:, 5:6]).then_inc(st["u_normed"], 1)
                for p in range(2):
                    act.wait_ge(h2_stored[p], 16 * TOK // 2)

            @block.vector
            def _(dve):
                for n, value in enumerate((SUBLN_EPS, LNX_EPS, EPS)):
                    nc.vector.memset(eps[:, n:n + 1], value).then_inc(const_done, 1)
                nc.vector.tensor_scalar(sub[:], table[:, par("subln_g")], 1.0 - LAMBDA_INIT, None,
                                        ALU.mult).then_inc(const_done, 1)
                dve.wait_ge(const_done, 4)
                for s, t in STAGES:
                    p = t % 2
                    if s == "heads":
                        wait(dve, "a_squared", t)
                        nc.vector.tensor_reduce(a_st[p][:, 0, :], heads(sq[:], 8), AX, ALU.add).then_inc(st["a_summed"], 1)
                        wait(dve, "y_added", t)
                        nc.vector.tensor_reduce(y_st[p][:, 0, :], heads(yf[p][:], 16), AX, ALU.add).then_inc(st["y_summed"], 1)
                        wait(dve, "y_summed", t)
                        nc.vector.tensor_scalar(y_st[p][:, 0, :], y_st[p][:, 0, :], 1.0 / N, None,
                                                ALU.mult).then_inc(st["y_mean"], 1)
                        wait(dve, "y_mean", t)
                        nc.vector.tensor_tensor(heads(yf[p][:], 16), heads(yf[p][:], 16),
                                                y_st[p][:, 0, :].unsqueeze(2).broadcast_to([P, 16, N]),
                                                ALU.subtract).then_inc(st["y_centred"], 1)
                        wait(dve, "a_rooted", t)
                        nc.vector.reciprocal(a_st[p][:, 2, :], a_st[p][:, 1, :]).then_inc(st["a_inverse"], 1)
                        wait(dve, "a_inverse", t)
                        nc.vector.tensor_tensor(heads(att[p][:], 8), heads(att[p][:], 8),
                                                a_st[p][:, 2, :].unsqueeze(2).broadcast_to([P, 8, P]),
                                                ALU.mult).then_inc(st["a_normed"], 1)
                        wait(dve, "y_squared", t)
                        nc.vector.tensor_reduce(y_st[p][:, 1, :], heads(sq_y[:], 16), AX, ALU.add).then_inc(st["y_varied"], 1)
                        wait(dve, "y_rooted", t)
                        nc.vector.reciprocal(y_st[p][:, 3, :], y_st[p][:, 2, :]).then_inc(st["y_inverse"], 1)
                        wait(dve, "y_inverse", t)
                        nc.vector.tensor_tensor(heads(yf[p][:], 16), heads(yf[p][:], 16),
                                                y_st[p][:, 3, :].unsqueeze(2).broadcast_to([P, 16, N]),
                                                ALU.mult).then_inc(st["y_normed"], 1)
                    elif s == "merge":
                        wait(dve, "a_turned", t)
                        dve.wait_ge(fm_here[p], 64 * (t // 2) + 64)
                        nc.vector.scalar_tensor_tensor(ma[:], tiles(ps_a[:]), sub[:], fm["gate_a"][p][:], ALU.mult,
                                                       ALU.mult).then_inc(st["ma"], 1)
                        wait(dve, "y_turned", t)
                        nc.vector.tensor_tensor(mr[:], tiles(ps_y[:]), columns("lnx_g"), ALU.mult).then_inc(st["mr_scaled"], 1)
                        wait(dve, "mr_scaled", t)
                        wait(dve, "bonus_shifted", t)
                        nc.vector.tensor_tensor(mr[:], mr[:], fm["bonus_v"][p][:], ALU.add).then_inc(st["mr_shifted"], 1)
                        wait(dve, "mr_shifted", t)
                        wait(dve, "gated", t)
                        nc.vector.tensor_tensor(mr[:], mr[:], fm["g"][p][:], ALU.mult).then_inc(st["mr"], 1)
                        wait(dve, "mr", t)
                        wait(dve, "projected", t - 2)
                        nc.vector.tensor_tensor(mT[p][:], ma[:], mr[:], ALU.add).then_inc(st["merged"], 1)
                    elif s == "mix":
                        wait(dve, "m_rooted", t)
                        nc.vector.reciprocal(m_st[p][:, 2:3], m_st[p][:, 1:2]).then_inc(st["m_inverse"], 1)
                        wait(dve, "m_inverse", t)
                        wait(dve, "u_normed", t - 2)
                        if t >= 2:
                            dve.wait_ge(h2_stored[p], 16 * (t // 2))
                        if t == 0:
                            dve.wait_ge(consts, 32)
                        nc.vector.scalar_tensor_tensor(h2[p][:], ps_m[:], m_st[p][:, 2:3], gain[:], ALU.mult,
                                                       ALU.mult).then_inc(st["m_normed"], 1)
                    elif s == "norm":
                        wait(dve, "h_rooted", t)
                        nc.vector.reciprocal(m_st[p][:, 5:6], m_st[p][:, 4:5]).then_inc(st["h_inverse"], 1)
                    elif s == "turn":
                        wait(dve, "u_turned", t)
                        nc.vector.tensor_tensor(u2T[:, :, t * P:(t + 1) * P], tiles(ps_u[:]), columns("pre_ffn_g"),
                                                ALU.mult).then_inc(st["u_kept"], 1)


HALVES = [(0, 512), (512, 512)]


def ffn_hidden(nc, sems, w_in, w_down, u2T, hidden, down):
    with ExitStack() as ctx:
        sb = lambda n, s: ctx.enter_context(nc.sbuf_tensor(n, s, F32))
        sem = lambda n: sems.enter_context(nc.semaphore(n))
        wt = [[sb(f"fh_w{j}{b}", [P, KC, P]) for b in range(2)] for j in range(2)]
        act_g = [sb(f"fh_act{b}", [P, SEQ]) for b in range(2)]
        ps = [[ctx.enter_context(nc.psum_tensor(f"fh_ps{j}{b}", [P, SEQ], F32)) for b in range(2)] for j in range(2)]
        w_here = [[sem(f"fh_w_here{j}{b}") for b in range(2)] for j in range(2)]
        made = [sem(f"fh_made{j}") for j in range(2)]
        silu_done, hidden_done = sem("fh_silu"), sem("fh_hidden")
        down_here = sem("fh_down_here")
        down_tiles = down.shape[1]

        with nc.Block() as block:
            @block.sync
            def _(sp):
                for sm in (*made, silu_done, hidden_done):
                    sp.sem_inc(sm, 2)
                with sp.Fori(0, FT // 2) as i:
                    for b in range(2):
                        for j in range(2):
                            sp.wait_ge(made[j], 2 * i + b + 1)
                            sp.dma_start(wt[j][b][:], w_in[2 * i + b, j]).then_inc(w_here[j][b], 16)

            @block.gpsimd
            def _(pool):
                pool.dma_start(down[:], w_down[:, 0:down_tiles, :]).then_inc(down_here, 16)
                pool.wait_ge(down_here, 16)

            @block.tensor
            def _(pe):
                with pe.Fori(0, FT // 2) as i:
                    for b in range(2):
                        for j in range(2):
                            pe.wait_ge(w_here[j][b], 16 * i + 16)
                            pe.wait_ge((silu_done, hidden_done)[j], 2 * i + b + 1)
                            for c, width in HALVES:
                                for k in range(KC):
                                    ins = nc.tensor.matmul(ps[j][b][:, c:c + width], wt[j][b][:, k, :], u2T[:, k, c:c + width],
                                                           start=(k == 0), stop=(k == KC - 1))
                            ins.then_inc(made[j], 1)

            @block.scalar
            def _(act):
                with act.Fori(0, FT // 2) as i:
                    for b in range(2):
                        act.wait_ge(made[0], 2 * i + b + 3)
                        act.wait_ge(hidden_done, 2 * i + b + 1)
                        nc.scalar.activation(act_g[b][:], ps[0][b][:], ACT.Silu).then_inc(silu_done, 1)

            @block.vector
            def _(dve):
                with dve.Fori(0, FT // 2) as i:
                    for b in range(2):
                        dve.wait_ge(silu_done, 2 * i + b + 3)
                        dve.wait_ge(made[1], 2 * i + b + 3)
                        nc.vector.tensor_tensor(hidden[:, 2 * i + b, :], ps[1][b][:], act_g[b][:],
                                                ALU.mult).then_inc(hidden_done, 1)


def ffn_down(nc, sems, w_down, h2_d, post_g, hidden, down, space, out):
    with ExitStack() as ctx:
        sb = lambda n, s: ctx.enter_context(nc.sbuf_tensor(n, s, F32))
        sem = lambda n: sems.enter_context(nc.semaphore(n))
        have = down.shape[1]
        more = sb("fd_more", [P, FT - have - KC, D])
        gain = sb("fd_gain", [P, D])
        eps = sb("fd_eps", [P, 1])
        h2 = [sb(f"fd_h2{p}", [P, D]) for p in range(2)]
        f = sb("fd_f", [P, D])
        sq = sb("fd_sq", [P, D])
        st = [sb(f"fd_st{p}", [P, 3]) for p in range(2)]
        ps = [ctx.enter_context(nc.psum_tensor(f"fd_ps{p}", [P, D], F32)) for p in range(2)]
        rest_here, gain_here, eps_set = sem("fd_rest_here"), sem("fd_gain_here"), sem("fd_eps_set")
        h2_here = [sem(f"fd_h2_here{p}") for p in range(2)]
        out_stored = [sem(f"fd_out_stored{p}") for p in range(2)]
        made, squared, rooted, inverse, normed, added = (sem(f"fd_{n}") for n in (
            "made", "squared", "rooted", "inverse", "normed", "added"))

        with nc.Block() as block:
            @block.sync
            def _(sp):
                for k in range(KC):
                    sp.dma_start(space[:, k, :], w_down[:, have + k, :]).then_inc(rest_here, 16)
                sp.dma_start(more[:], w_down[:, have + KC:, :]).then_inc(rest_here, 16)
                sp.dma_start(gain[:], post_g.broadcast_to([P, D])).then_inc(gain_here, 16)
                for t in range(TOK):
                    p = t % 2
                    if t >= 2:
                        sp.wait_ge(out_stored[p], 16 * (t // 2))
                    sp.dma_start(h2[p][:], h2_d[t * P:(t + 1) * P, :]).then_inc(h2_here[p], 16)

            @block.tensor
            def _(pe):
                for t in range(TOK):
                    p = t % 2
                    if t >= 2:
                        pe.wait_ge(normed, t - 1)
                    for k in range(FT):
                        if k == have and t == 0:
                            pe.wait_ge(rest_here, 16 * (KC + 1))
                        w = down[:, k, :] if k < have else space[:, k - have, :] if k < have + KC else more[:, k - have - KC, :]
                        for c, width in HALVES:
                            ins = nc.tensor.matmul(ps[p][:, c:c + width], hidden[:, k, t * P:(t + 1) * P], w[:, c:c + width],
                                                   start=(k == 0), stop=(k == FT - 1))
                    ins.then_inc(made, 1)

            @block.scalar
            def _(act):
                act.wait_ge(eps_set, 1)
                for t in range(TOK):
                    p = t % 2
                    act.wait_ge(made, t + 1)
                    nc.scalar.activation(sq[:], ps[p][:], ACT.Square, accum_out=st[p][:, 0:1]).then_inc(squared, 1)
                    act.wait_ge(squared, t + 1)
                    nc.scalar.activation(st[p][:, 1:2], st[p][:, 0:1], ACT.Sqrt, bias=eps[:], scale=1.0 / D).then_inc(rooted, 1)
                    act.wait_ge(added, t + 1)
                    act.dma_start(out[t * P:(t + 1) * P, :], h2[p][:]).then_inc(out_stored[p], 16)
                for p in range(2):
                    act.wait_ge(out_stored[p], 16 * TOK // 2)

            @block.vector
            def _(dve):
                nc.vector.memset(eps[:], EPS).then_inc(eps_set, 1)
                dve.wait_ge(gain_here, 16)
                for t in range(TOK):
                    p = t % 2
                    dve.wait_ge(rooted, t + 1)
                    nc.vector.reciprocal(st[p][:, 2:3], st[p][:, 1:2]).then_inc(inverse, 1)
                    dve.wait_ge(inverse, t + 1)
                    if t >= 1:
                        dve.wait_ge(added, t)
                    nc.vector.scalar_tensor_tensor(f[:], ps[p][:], st[p][:, 2:3], gain[:], ALU.mult, ALU.mult).then_inc(normed, 1)
                    dve.wait_ge(normed, t + 1)
                    dve.wait_ge(h2_here[p], 16 * (t // 2) + 16)
                    nc.vector.tensor_tensor(h2[p][:], f[:], h2[p][:], ALU.add).then_inc(added, 1)


def tail(nc, sems, space, a, att_d, y_d, kept_d, h2_d, ident, table):
    sb = lambda n, s: space.enter_context(nc.sbuf_tensor(n, s, F32))
    u2T = sb("u2T", [P, KC, SEQ])
    merge_and_mix(nc, sems, a["x"], att_d, y_d, kept_d, a["w_out"], a["post_mix_g"], ident, table, u2T, h2_d)
    hidden, down = sb("hidden", [P, FT, SEQ]), sb("down", [P, DOWN_EARLY, D])
    ffn_hidden(nc, sems, a["w_ffn_in"], a["w_ffn_out"], u2T, hidden, down)
    ffn_down(nc, sems, a["w_ffn_out"], h2_d, a["post_ffn_g"], hidden, down, u2T, a["out"])


class fresh_semaphores:

    def __init__(self, nc):
        self.nc, self.taken = nc, []

    def __enter__(self):
        return self

    def enter_context(self, context):
        handle = context.__enter__()
        self.taken.append(handle)
        return handle

    def __exit__(self, *error):
        if error[0] is None:
            self.nc.clear_and_free_semaphores(self.taken)
            self.nc.all_engine_barrier()


def build(nc, a):
    dram = lambda name, shape: nc.dram_tensor(name, shape, F32).ap()
    prep_d = dram("s_prep", [HEADS, NT, P, REC])
    kept_d = dram("s_kept", [len(KEPT), HEADS, P, T])
    att_d = dram("s_att", [T, D])
    y_d = dram("s_y", [2, T, D])
    h2_d = dram("s_h2", [SEQ, D])
    with ExitStack() as whole:
        sb = lambda where, n, s: where.enter_context(nc.sbuf_tensor(n, s, F32))
        ident, ones = sb(whole, "ident", [P, P]), sb(whole, "ones", [P, P])
        table, more = sb(whole, "table", [P, NPAR]), sb(whole, "more", [P, 94])
        nlam = sb(whole, "nlam", [P, 1])
        with fresh_semaphores(nc) as sems:
            load_constants(nc, sems, a["ident"], a["ones"], a["params"], ident, ones, table, more)
            with ExitStack() as part:
                uT = sb(part, "uT", [P, KC, T])
                lor, gl, gl2 = sb(part, "lor", [P, T]), sb(part, "gl", [P, T]), sb(part, "gl2", [GL - P, T])
                norm_and_turn(nc, sems, a["meta_tokens"], a["x"], ident, table, uT)
                low_rank_inputs(nc, sems, a["w_lora"], uT, more, lor, gl, gl2)
                project_and_prepare(nc, sems, a["w_main"], a["w_low"], uT, ones, table, more, lor, gl, gl2, prep_d, kept_d)
        with fresh_semaphores(nc) as sems:
            learned_lambda(nc, sems, a["lq1"], a["lk1"], a["lq2"], a["lk2"], nlam)
            attention(nc, sems, kept_d, a["cos"], a["sin"], ident, nlam, att_d)
            recurrence(nc, sems, prep_d, a["masks"], ident, y_d)
        tail(nc, whole, whole, a, att_d, y_d, kept_d, h2_d, ident, table)


def kernel(x, meta_tokens, pre_mix_g, w_in, att_lq1, att_lk1, att_lq2, att_lk2, att_subln_g, rwkv_mu, rwkv_w0,
           rwkv_w_up, rwkv_a0, rwkv_a_up, rwkv_g_up, rwkv_k_k, rwkv_k_a, rwkv_r_k, rwkv_lnx_g, rwkv_lnx_b, w_out,
           post_mix_g, pre_ffn_g, w_ffn_in, w_ffn_out, post_ffn_g):
    import concourse.bacc as bacc
    from concourse.bass_utils import run_bass_kernel_spmd

    arr = lambda v: np.asarray(v)[0]
    w = arr(w_in)

    def feature_tiles(m, first, n):
        return m[:, first:first + n * P].reshape(-1, P, n, P).transpose(2, 1, 0, 3)

    starts = {"r": RW0, "k": RW0 + D, "v": RW0 + 2 * D, "att_q": 0, "att_k": D, "att_v": 2 * D, "gate_a": GATE0,
              "gate_r": GATE0 + D}
    w_main = np.stack([feature_tiles(w, starts[n], HEADS) for n in MAIN], 1)
    w_lora = w[:, LORA0:GATE0].reshape(KC, P, GATE0 - LORA0).transpose(1, 0, 2)
    w_low = np.zeros((HEADS, P, 6, P), w.dtype)
    w_up = arr(rwkv_w_up).reshape(2, N, HEADS, P)
    a_up = arr(rwkv_a_up).reshape(2, N, HEADS, P)
    g_up = arr(rwkv_g_up).reshape(GL, HEADS, P)
    for z in range(2):
        w_low[:, :N, z] = w_up[z].transpose(1, 0, 2)
        w_low[:, N:, 2 + z] = a_up[z].transpose(1, 0, 2)
    w_low[:, :, 4] = g_up[:P].transpose(1, 0, 2)
    w_low[:, :GL - P, 5] = g_up[P:].transpose(1, 0, 2)
    columns = lambda v: np.reshape(v, (-1, P)).T
    mu = arr(rwkv_mu)
    mu_lora = np.zeros(3 * P, mu.dtype)
    mu_lora[:GATE0 - LORA0] = mu[3 * D:]
    params = np.concatenate([columns(v) for v in (
        mu[:3 * D], mu_lora, arr(rwkv_w0), arr(rwkv_a0), arr(rwkv_k_k), arr(rwkv_k_a), arr(rwkv_r_k), arr(rwkv_lnx_g),
        arr(rwkv_lnx_b), arr(pre_mix_g), arr(post_mix_g), arr(pre_ffn_g), arr(post_ffn_g), arr(att_subln_g))], 1)
    inv = (1.0 / (np.float32(10000.0) ** (np.arange(0, DQ, 2, dtype=np.float32) / np.float32(DQ)))).astype(np.float32)
    angle = np.arange(T, dtype=np.float32)[None, :] * inv[:, None]
    cos, sin = np.cos(angle), np.sin(angle)
    w1 = arr(w_ffn_in)
    ffn_in = np.stack([feature_tiles(w1, 0, FT), feature_tiles(w1, FFN, FT)], 1)
    arrays = {
        "x": np.asarray(x)[0], "meta_tokens": np.asarray(meta_tokens), "w_main": w_main, "w_lora": w_lora,
        "w_low": w_low, "params": params, "ident": np.eye(P, dtype=np.float32),
        "ones": np.kron(np.eye(2, dtype=np.float32), np.ones((N, N), np.float32)), "masks": recurrence_masks(),
        "lq1": np.asarray(att_lq1), "lk1": np.asarray(att_lk1), "lq2": np.asarray(att_lq2), "lk2": np.asarray(att_lk2),
        "cos": np.concatenate([cos] * 4, 0), "sin": np.concatenate([-sin, sin, -sin, sin], 0),
        "w_out": arr(w_out).reshape(KC, P, D).transpose(1, 0, 2), "post_mix_g": np.asarray(post_mix_g),
        "w_ffn_in": ffn_in, "w_ffn_out": arr(w_ffn_out).reshape(FT, P, D).transpose(1, 0, 2),
        "post_ffn_g": np.asarray(post_ffn_g),
    }
    nc = bacc.Bacc("TRN2", target_bir_lowering=False, num_devices=1)
    ins, aps = {}, {}
    for name, v in arrays.items():
        v = np.ascontiguousarray(v)
        ins[f"in_{name}"] = v
        aps[name] = nc.dram_tensor(f"in_{name}", v.shape, mybir.dt.from_np(v.dtype), kind="ExternalInput").ap()
    aps["out"] = nc.dram_tensor("out_0", [SEQ, D], F32, kind="ExternalOutput").ap()
    build(nc, aps)
    result = run_bass_kernel_spmd(nc, [ins], core_ids=[0])
    return result.results[0]["out_0"].reshape(1, SEQ, D)
```

```python
import math
from contextlib import ExitStack

import numpy as np

import concourse.bass as bass
from concourse import mybir

F32 = mybir.dt.float32
ALU = mybir.AluOpType
ACT = mybir.ActivationFunctionType
AX = mybir.AxisListType.X

P = 128
D = 1024
KC = D // P
META = 16
SEQ = 1024
T = SEQ + META
EPS = 1e-6

L = 104
NT = T // L
NB = 4
NW = T // NB

HEADS = 8
DQ = 64
N = 64
RW0 = 3 * D
LORA0 = RW0 + 3 * D
GL = 160
GATE0 = LORA0 + 2 * N + GL
COLS = GATE0 + 2 * D
DECAY = math.exp(-0.5)

PAR = {}
for _name, _n in (("mu", 24), ("mu_lora", 3), ("w0", 16), ("a0", 16), ("k_k", 8), ("k_a", 8), ("r_k", 8),
                  ("lnx_g", 8), ("lnx_b", 8), ("pre_mix_g", 8), ("post_mix_g", 8), ("pre_ffn_g", 8),
                  ("post_ffn_g", 8), ("subln_g", 1)):
    PAR[_name] = sum(n for _, n in PAR.values()), _n
NPAR = sum(n for _, n in PAR.values())


def par(name, i=0):
    return bass.ds(PAR[name][0] + i, 1)

FFN = 2816
FT = FFN // P


def cols(bank_tile):
    return bank_tile[:, :, 0:NW]


def banked(ap):
    return ap.rearrange("p (n w) -> p n w", n=NB)


def norm_and_turn(nc, sems, meta, x, ident, table, uT):
    with ExitStack() as ctx:
        sb = lambda n, s: ctx.enter_context(nc.sbuf_tensor(n, s, F32))
        sem = lambda n: sems.enter_context(nc.semaphore(n))
        xt = [sb(f"n1_x{s}", [L, D]) for s in range(2)]
        un = [sb(f"n1_u{s}", [L, D]) for s in range(2)]
        sq = sb("n1_sq", [L, D])
        ms = [sb(f"n1_ms{s}", [L, 4]) for s in range(2)]
        eps = sb("n1_eps", [P, 1])
        ps = ctx.enter_context(nc.psum_tensor("n1_ps", [P, 2, 2, 512], F32))
        eps_set = sem("n1_eps_set")
        x_in = [sem(f"n1_x_in{s}") for s in range(2)]
        summed = sem("n1_summed")
        rooted = sem("n1_rooted")
        chain = sem("n1_chain")
        normed = sem("n1_normed")
        u_turned = sem("n1_u_turned")
        u_kept = sem("n1_u_kept")

        def turned(s, half):
            return ps[:, s, half, 0:4 * L].rearrange("p (k t) -> p k t", k=4)

        with nc.Block() as block:
            @block.sync
            def _(sp):
                sp.sem_inc(x_in[1], 16)
                for t in range(NT):
                    s = t % 2
                    if t >= 2:
                        sp.wait_ge(normed, t - 1)
                    if t == 0:
                        sp.dma_start(xt[0][0:META, :], meta).then_inc(x_in[0], 16)
                        sp.dma_start(xt[0][META:L, :], x[0:L - META, :]).then_inc(x_in[0], 16)
                    else:
                        sp.dma_start(xt[s][:], x[t * L - META:(t + 1) * L - META, :]).then_inc(x_in[s], 16)

            @block.scalar
            def _(act):
                act.wait_ge(eps_set, 1)
                with act.Fori(0, NT // 2) as i:
                    for s in range(2):
                        act.wait_ge(x_in[s], 16 * i + 32)
                        nc.scalar.activation(sq[:], xt[s][:], ACT.Square,
                                             accum_out=ms[s][:, 0:1]).then_inc(summed, 1)
                        act.wait_ge(summed, 2 * i + s + 1)
                        nc.scalar.activation(ms[s][:, 1:2], ms[s][:, 0:1], ACT.Sqrt, bias=eps[0:L, :],
                                             scale=1.0 / D).then_inc(rooted, 1)

            @block.vector
            def _(dve):
                nc.vector.memset(eps[:], EPS).then_inc(eps_set, 1)
                with dve.Fori(0, NT // 2) as i:
                    for s in range(2):
                        dve.wait_ge(rooted, 2 * i + s + 1)
                        nc.vector.reciprocal(ms[s][:, 2:3], ms[s][:, 1:2]).then_inc(chain, 1)
                        dve.wait_ge(chain, 2 * i + s + 1)
                        dve.wait_ge(u_turned, 2 * i + s + 1)
                        nc.vector.tensor_scalar(un[s][:], xt[s][:], ms[s][:, 2:3], None,
                                                ALU.mult).then_inc(normed, 1)
                    for s in range(2):
                        dve.wait_ge(u_turned, 2 * i + s + 3)
                        for half in range(2):
                            out = uT[:, 4 * half:4 * half + 4, bass.ts(2 * i + s, L)]
                            at = PAR["pre_mix_g"][0] + 4 * half
                            gain = table[:, at:at + 4].unsqueeze(2).broadcast_to([P, 4, L])
                            nc.vector.tensor_tensor(out, turned(s, half), gain, ALU.mult).then_inc(u_kept, 1)

            @block.tensor
            def _(pe):
                pe.sem_inc(u_turned, 2)
                pe.sem_inc(u_kept, 4)
                with pe.Fori(0, NT // 2) as i:
                    for s in range(2):
                        pe.wait_ge(normed, 2 * i + s + 1)
                        pe.wait_ge(u_kept, 4 * i + 2 * s + 2)
                        for k in range(KC):
                            ins = nc.tensor.transpose(turned(s, k // 4)[:, k % 4, :],
                                                      un[s][:, k * P:(k + 1) * P], ident[0:L, 0:L])
                        ins.then_inc(u_turned, 1)


def load_constants(nc, sems, ident_d, ones_d, table_d, ident, ones, table, more):
    here = sems.enter_context(nc.semaphore("c_here"))
    done = sems.enter_context(nc.semaphore("c_done"))
    with nc.Block() as block:
        @block.sync
        def _(sp):
            sp.dma_start(ident[:], ident_d).then_inc(here, 16)
            sp.dma_start(ones[:], ones_d).then_inc(here, 16)
            sp.dma_start(table[:], table_d).then_inc(here, 16)

        @block.vector
        def _(dve):
            dve.wait_ge(here, 48)
            mu = table[:, 0:27]
            nc.vector.tensor_scalar(more[:, 0:27], mu, -1.0, 1.0, ALU.mult, ALU.add).then_inc(done, 1)
            nc.vector.tensor_scalar(more[:, 27:54], mu, 0.5, None, ALU.mult).then_inc(done, 1)
            nc.vector.tensor_scalar(more[:, 54:86], table[:, 27:59], 0.5, None, ALU.mult).then_inc(done, 1)
            k_a = table[:, PAR["k_a"][0]:PAR["k_a"][0] + 8]
            nc.vector.tensor_scalar(more[:, 86:94], k_a, -1.0, 1.0, ALU.mult, ALU.add).then_inc(done, 1)
            dve.wait_ge(done, 4)


def keep(i):
    return bass.ds(i, 1)


def half_mu(i):
    return bass.ds(27 + i, 1)


def half_bias(i):
    return bass.ds(54 + i, 1)


def one_minus_ka(i):
    return bass.ds(86 + i, 1)


def low_rank_inputs(nc, sems, w_lora, uT, more, lor, gl, gl2):
    with ExitStack() as ctx:
        sb = lambda n, s: ctx.enter_context(nc.sbuf_tensor(n, s, F32))
        sem = lambda n: sems.enter_context(nc.semaphore(n))
        W = 2 * N + GL
        w = sb("lr_w", [P, KC, W])
        raw = [sb(f"lr_raw{j}", [P, T + 2]) for j in range(3)]
        kept = [sb(f"lr_kept{j}", [P, T]) for j in range(3)]
        shifted = [sb(f"lr_shifted{j}", [P, T]) for j in range(3)]
        ps = [ctx.enter_context(nc.psum_tensor(f"lr_ps{s}", [P, NB, 512], F32)) for s in range(2)]
        w_here, product, copied, padded = sem("lr_w_here"), sem("lr_product"), sem("lr_copied"), sem("lr_padded")
        scaled, summed, mixed, done = sem("lr_scaled"), sem("lr_summed"), sem("lr_mixed"), sem("lr_done")
        rows = [P, P, GL - P]
        out = [lor, gl, gl2]

        with nc.Block() as block:
            @block.sync
            def _(sp):
                sp.dma_start(w[:], w_lora).then_inc(w_here, 16)

            @block.tensor
            def _(pe):
                pe.wait_ge(w_here, 16)
                for j, m in enumerate(rows):
                    if j == 2:
                        pe.wait_ge(scaled, 1)
                    for n in range(NB):
                        for k in range(KC):
                            ins = nc.tensor.matmul(ps[j % 2][0:m, n, 0:NW], w[:, k, j * P:j * P + m],
                                                   uT[:, k, n * NW:(n + 1) * NW], start=(k == 0), stop=(k == KC - 1))
                    ins.then_inc(product, 1)

            @block.scalar
            def _(act):
                for j, m in enumerate(rows):
                    act.wait_ge(product, j + 1)
                    nc.scalar.copy(banked(raw[j][0:m, 1:T + 1]), ps[j % 2][0:m, :, 0:NW]).then_inc(copied, 1)
                    nc.scalar.activation(banked(kept[j][0:m, :]), ps[j % 2][0:m, :, 0:NW], ACT.Copy,
                                         scale=more[0:m, keep(24 + j)]).then_inc(scaled, 1)
                act.wait_ge(mixed, 1)
                nc.scalar.activation(lor[0:N, :], lor[0:N, :], ACT.Tanh).then_inc(done, 1)
                act.wait_ge(mixed, 3)
                nc.scalar.activation(gl[:], gl[:], ACT.Sigmoid).then_inc(done, 1)
                nc.scalar.activation(gl2[0:GL - P, :], gl2[0:GL - P, :], ACT.Sigmoid).then_inc(done, 1)
                act.wait_ge(done, 3)

            @block.vector
            def _(dve):
                for j in range(3):
                    nc.vector.memset(raw[j][:, 0:1], 0.0).then_inc(padded, 1)
                    nc.vector.memset(raw[j][:, T + 1:T + 2], 0.0).then_inc(padded, 1)
                dve.wait_ge(padded, 6)
                for j, m in enumerate(rows):
                    dve.wait_ge(copied, j + 1)
                    nc.vector.tensor_tensor(shifted[j][0:m, :], raw[j][0:m, 0:T], raw[j][0:m, 2:T + 2],
                                            ALU.add).then_inc(summed, 1)
                    dve.wait_ge(summed, j + 1)
                    dve.wait_ge(scaled, j + 1)
                    nc.vector.scalar_tensor_tensor(out[j][0:m, :], shifted[j][0:m, :], more[0:m, half_mu(24 + j)],
                                                   kept[j][0:m, :], ALU.mult, ALU.add).then_inc(mixed, 1)


TURNS = ["r", "k", "v", "w0", "w1", "a0", "a1", "g", "att_q", "att_k", "kk_sum", "bonus", "att_v", "gate_a", "gate_r"]
MAIN = ["r", "k", "v", "att_q", "att_k", "att_v", "gate_a", "gate_r"]
PER = [sum(1 for t in range(len(TURNS)) if t % 2 == s) for s in range(2)]
REC_AT = {"log0": 0, "kd0": L + 1, "nb0": 2 * L + 1, "r": 3 * L + 1, "v": 4 * L + 1, "kk": 5 * L + 1,
          "kd1": 6 * L + 1, "nb1": 7 * L + 1, "log1": 8 * L + 1}
REC = 9 * L + 2
HALF_REC = 6 * L + 1
KEPT = ["att_q", "att_k", "att_v", "gate_a", "gate_r", "g", "bonus_v"]


def project_and_prepare(nc, sems, w_main, w_low, uT, ones, table, more, lor, gl, gl2, prep_d, kept_d):
    with ExitStack() as ctx:
        sb = lambda n, s: ctx.enter_context(nc.sbuf_tensor(n, s, F32))
        sem = lambda n: sems.enter_context(nc.semaphore(n))
        wt = [sb(f"pp_w{s}", [P, KC, P]) for s in range(2)]
        wl = sb("pp_wl", [P, 6, P])
        raw = {x: sb(f"pp_raw_{x}", [P, T + 2]) for x in "rkv"}
        scaled = {x: sb(f"pp_scaled_{x}", [P, T]) for x in "rkv"}
        neighbours = sb("pp_neighbours", [P, T])
        th = [sb(f"pp_th{j}", [P, T]) for j in range(4)]
        kmix = sb("pp_kmix", [P, T])
        kk = sb("pp_kk", [P, T])
        sq = sb("pp_sq", [P, T])
        tmp = sb("pp_tmp", [P, T])
        rk = sb("pp_rk", [P, T])
        bv = sb("pp_bv", [P, T])
        ob = [sb(f"pp_ob{s}", [P, T]) for s in range(2)]
        sums = sb("pp_sums", [P, T])
        within = sb("pp_within", [P, T])
        prep = sb("pp_prep", [P, NT, REC])
        ps = [ctx.enter_context(nc.psum_tensor(f"pp_ps{s}", [P, NB, 512], F32)) for s in range(2)]

        filled = [sem(f"pp_filled{s}") for s in range(2)]
        emptied = [sem(f"pp_emptied{s}") for s in range(2)]
        w_here = [sem(f"pp_w_here{s}") for s in range(2)]
        wl_here = sem("pp_wl_here")
        padded, ready = sem("pp_padded"), sem("pp_ready")
        stored = [sem(f"pp_stored{s}") for s in range(2)]
        prep_stored = sem("pp_prep_stored")
        bonus_stored = sem("pp_bonus_stored")
        once = {}
        for name in ("raw_r", "raw_k", "raw_v", "summed_r", "summed_k", "summed_v", "mixed_r", "mixed_k", "mixed_v",
                     "kk_raw", "kk_squared", "lw_0", "lw_1", "log_sum_0", "log_sum_1", "log_0", "log_1",
                     "log_first", "a_0", "a_1", "kf_0", "kf_1", "kd_0", "kd_1", "kd_both",
                     "rk", "kk_root", "kk_inverse", "kk_done", "b_0", "b_1", "bonus_done"):
            once[name] = sem(f"pp_{name}")
        before = lambda i: i + 1
        now = lambda i: i + 2

        def count(i, turn, s):
            return PER[s] * i + PER[s] + turn // 2 + 1

        def slot(name):
            turn = TURNS.index(name)
            return turn, turn % 2

        def out(name):
            return prep[:, :, REC_AT[name]:REC_AT[name] + L]

        by_chunk = lambda ap: ap.rearrange("p (c t) -> p c t", c=NT)

        with nc.Block() as block:
            @block.sync
            def _(sp):
                for name in once:
                    sp.sem_inc(once[name], 1)
                sp.sem_inc(prep_stored, 16)
                with sp.Fori(0, HEADS) as i:
                    sp.wait_ge(filled[1], count(i - 1, TURNS.index("g"), 1))
                    sp.dma_start(wl[:], w_low[i]).then_inc(wl_here, 16)
                    for j, name in enumerate(MAIN):
                        was, s = slot(MAIN[j - 2])
                        sp.wait_ge(filled[s], count(i - (j < 2), was, s))
                        sp.dma_start(wt[j % 2][:], w_main[i, j]).then_inc(w_here[j % 2], 16)
                    for done in ("mixed_r", "mixed_v", "log_0", "log_1", "log_first", "kd_0", "kd_1", "kk_done", "b_0",
                                 "b_1"):
                        sp.wait_ge(once[done], now(i))
                    sp.dma_start(prep_d[i].rearrange("c p a -> p c a"), prep[:]).then_inc(prep_stored, 16)
                sp.wait_ge(prep_stored, 16 * HEADS + 16)

            @block.tensor
            def _(pe):
                for s in range(2):
                    pe.sem_inc(filled[s], PER[s])
                with pe.Fori(0, HEADS) as i:
                    pe.wait_ge(wl_here, 16 * i + 16)
                    for turn, name in enumerate(TURNS):
                        s = turn % 2
                        pe.wait_ge(emptied[s], count(i, turn, s) - 1)
                        if name in MAIN:
                            j = MAIN.index(name)
                            pe.wait_ge(w_here[j % 2], 64 * i + 16 * (j // 2) + 16)
                            parts = [(wt[j % 2][:, k, :], uT[:, k, :]) for k in range(KC)]
                        elif name == "g":
                            parts = [(wl[:, 4, :], gl[:]), (wl[0:GL - P, 5, :], gl2[:])]
                        elif name == "kk_sum":
                            pe.wait_ge(once["kk_squared"], now(i))
                            parts = [(ones[:], sq[:])]
                        elif name == "bonus":
                            pe.wait_ge(once["rk"], now(i))
                            parts = [(ones[:], rk[:])]
                        else:
                            parts = [(wl[:, ["w0", "w1", "a0", "a1"].index(name), :], lor[:])]
                        for n in range(NB):
                            for k, (weights, moving) in enumerate(parts):
                                ins = nc.tensor.matmul(ps[s][:, n, 0:NW], weights, moving[:, n * NW:(n + 1) * NW],
                                                       start=(k == 0), stop=(k == len(parts) - 1))
                        ins.then_inc(filled[s], 1)

            @block.scalar
            def _(act):
                for s in range(2):
                    act.sem_inc(emptied[s], PER[s])
                    act.sem_inc(stored[s], 16)
                act.sem_inc(bonus_stored, 16)
                act.wait_ge(padded, 6)
                with act.Fori(0, HEADS) as i:
                    def fill(name):
                        turn, s = slot(name)
                        act.wait_ge(filled[s], count(i, turn, s))
                        return s

                    def take_mixed(x):
                        s = fill(x)
                        act.wait_ge(once[f"summed_{x}"], before(i))
                        nc.scalar.copy(banked(raw[x][:, 1:T + 1]), cols(ps[s])).then_inc(once[f"raw_{x}"], 1)
                        act.wait_ge(once[f"mixed_{x}"], before(i))
                        nc.scalar.activation(banked(scaled[x][:]), cols(ps[s]), ACT.Copy,
                                             scale=more[:, keep("rkv".index(x) * HEADS + i)]).then_inc(emptied[s], 1)

                    def keep_turn(name, n):
                        s = fill(name)
                        act.wait_ge(stored[n % 2], 48 * i + 16 * (n // 2) + 16)
                        func = ACT.Sigmoid if name.startswith("gate") else ACT.Copy
                        nc.scalar.activation(banked(ob[n % 2][:]), cols(ps[s]), func).then_inc(emptied[s], 1)
                        act.wait_ge(emptied[s], count(i, TURNS.index(name), s))
                        act.dma_start(kept_d[KEPT.index(name), i], ob[n % 2][:]).then_inc(stored[n % 2], 16)

                    for x in "rkv":
                        take_mixed(x)
                    act.wait_ge(once["mixed_k"], now(i))
                    act.wait_ge(once["kk_done"], before(i))
                    nc.scalar.activation(kk[:], kmix[:], ACT.Copy, scale=table[:, par("k_k", i)]).then_inc(once["kk_raw"], 1)
                    act.wait_ge(once["kk_raw"], now(i))
                    act.wait_ge(filled[0], count(i - 1, TURNS.index("kk_sum"), 0))
                    nc.scalar.activation(sq[:], kk[:], ACT.Square).then_inc(once["kk_squared"], 1)
                    for j, name in enumerate(("w0", "w1", "a0", "a1")):
                        s = fill(name)
                        act.wait_ge(once[("kd_0", "kd_1", "b_0", "b_1")[j]], before(i))
                        nc.scalar.activation(banked(th[j][:]), cols(ps[s]), ACT.Tanh, scale=0.5,
                                             bias=more[:, half_bias(8 * j + i)]).then_inc(emptied[s], 1)
                    keep_turn("g", 0)
                    keep_turn("att_q", 1)
                    keep_turn("att_k", 2)
                    s = fill("bonus")
                    act.wait_ge(bonus_stored, 16 * i + 16)
                    nc.scalar.copy(banked(bv[:]), cols(ps[s])).then_inc(emptied[s], 1)
                    act.wait_ge(emptied[0], count(i, TURNS.index("kk_sum"), 0))
                    nc.scalar.activation(tmp[:], tmp[:], ACT.Sqrt).then_inc(once["kk_root"], 1)
                    keep_turn("att_v", 3)
                    act.wait_ge(once["bonus_done"], now(i))
                    act.dma_start(kept_d[KEPT.index("bonus_v"), i], bv[:]).then_inc(bonus_stored, 16)
                    keep_turn("gate_a", 4)
                    keep_turn("gate_r", 5)
                for s in range(2):
                    act.wait_ge(stored[s], 48 * HEADS + 16)
                act.wait_ge(bonus_stored, 16 * HEADS + 16)

            @block.gpsimd
            def _(pool):
                for x in "rkv":
                    nc.gpsimd.memset(raw[x][:, 0:1], 0.0).then_inc(padded, 1)
                    nc.gpsimd.memset(raw[x][:, T + 1:T + 2], 0.0).then_inc(padded, 1)
                pool.wait_ge(padded, 6)
                with pool.Fori(0, HEADS) as i:
                    for n, x in enumerate("rkv"):
                        pool.wait_ge(once[f"raw_{x}"], now(i))
                        pool.wait_ge(once[f"mixed_{'vrk'[n]}"], now(i) - (n == 0))
                        nc.gpsimd.tensor_tensor(neighbours[:], raw[x][:, 0:T], raw[x][:, 2:T + 2],
                                                ALU.add).then_inc(once[f"summed_{x}"], 1)

            @block.vector
            def _(dve):
                nc.vector.memset(within[:], 1.0).then_inc(ready, 1)
                nc.vector.memset(prep[:, :, REC_AT["log0"]:REC_AT["log0"] + 1], 0.0).then_inc(ready, 1)
                dve.wait_ge(ready, 2)
                nc.vector.memset(by_chunk(within[:])[:, :, 0:1], 0.0).then_inc(ready, 1)
                dve.wait_ge(ready, 3)
                with dve.Fori(0, HEADS) as i:
                    def once_is(name):
                        dve.wait_ge(once[name], now(i))

                    def read(name):
                        turn, s = slot(name)
                        dve.wait_ge(emptied[s], count(i, turn, s))

                    dve.wait_ge(prep_stored, 16 * i + 16)
                    for n, (x, dst) in enumerate((("r", out("r")), ("k", by_chunk(kmix[:])), ("v", out("v")))):
                        once_is(f"summed_{x}")
                        read(x)
                        nc.vector.scalar_tensor_tensor(dst, by_chunk(neighbours[:]), more[:, half_mu(8 * n + i)],
                                                       by_chunk(scaled[x][:]), ALU.mult,
                                                       ALU.add).then_inc(once[f"mixed_{x}"], 1)
                    for z in range(2):
                        read(f"w{z}")
                        nc.vector.tensor_scalar(th[z][:], th[z][:], -0.5 * DECAY, -0.5 * DECAY,
                                                ALU.mult, ALU.add).then_inc(once[f"lw_{z}"], 1)
                        once_is(f"lw_{z}")
                        dve.wait_ge(once[f"log_{1 - z}"], now(i) - (z == 0))
                        nc.vector.tensor_tensor_scan(out=sums[:], data0=within[:], data1=th[z][:], initial=0.0,
                                                     op0=ALU.mult, op1=ALU.add).then_inc(once[f"log_sum_{z}"], 1)
                        once_is(f"log_sum_{z}")
                        if z == 0:
                            nc.vector.tensor_copy(prep[:, :, REC_AT["log0"] + 1:REC_AT["log0"] + 1 + L],
                                                  by_chunk(sums[:])).then_inc(once["log_0"], 1)
                        else:
                            total = by_chunk(sums[:])[:, :, L - 1:L]
                            nc.vector.tensor_scalar(prep[:, :, REC_AT["log1"]:REC_AT["log1"] + 1], total, -1.0, None,
                                                    ALU.mult).then_inc(once["log_first"], 1)
                            nc.vector.tensor_tensor(prep[:, :, REC_AT["log1"] + 1:REC_AT["log1"] + 1 + L],
                                                    by_chunk(sums[:]), total.broadcast_to([P, NT, L]),
                                                    ALU.subtract).then_inc(once["log_1"], 1)
                    for z in range(2):
                        a = th[2 + z]
                        read(f"a{z}")
                        nc.vector.tensor_scalar(a[:], a[:], 0.5, 0.5, ALU.mult, ALU.add).then_inc(once[f"a_{z}"], 1)
                        once_is(f"a_{z}")
                        nc.vector.tensor_scalar(th[z][:], a[:], table[:, par("k_a", i)], more[:, one_minus_ka(i)],
                                                ALU.mult, ALU.add).then_inc(once[f"kf_{z}"], 1)
                        once_is(f"kf_{z}")
                        nc.vector.tensor_tensor(out(f"kd{z}"), by_chunk(th[z][:]), by_chunk(kmix[:]),
                                                ALU.mult).then_inc(once[f"kd_{z}"], 1)
                    for z in range(2):
                        once_is(f"kd_{z}")
                    nc.vector.tensor_tensor(by_chunk(tmp[:]), out("kd0"), out("kd1"), ALU.add).then_inc(once["kd_both"], 1)
                    once_is("kd_both")
                    dve.wait_ge(filled[1], count(i - 1, TURNS.index("bonus"), 1))
                    nc.vector.scalar_tensor_tensor(by_chunk(rk[:]), by_chunk(tmp[:]), table[:, par("r_k", i)], out("r"),
                                                   ALU.mult, ALU.mult).then_inc(once["rk"], 1)
                    once_is("rk")
                    turn, s = slot("kk_sum")
                    dve.wait_ge(filled[s], count(i, turn, s))
                    nc.vector.tensor_scalar(banked(tmp[:]), cols(ps[s]), 1e-24, None, ALU.max).then_inc(emptied[s], 1)
                    once_is("kk_root")
                    nc.vector.reciprocal(tmp[:], tmp[:]).then_inc(once["kk_inverse"], 1)
                    once_is("kk_inverse")
                    nc.vector.tensor_tensor(out("kk"), by_chunk(kk[:]), by_chunk(tmp[:]), ALU.mult).then_inc(once["kk_done"], 1)
                    once_is("kk_done")
                    for z in range(2):
                        nc.vector.scalar_tensor_tensor(out(f"nb{z}"), out("kk"), -1.0, by_chunk(th[2 + z][:]), ALU.mult,
                                                       ALU.mult).then_inc(once[f"b_{z}"], 1)
                    read("bonus")
                    once_is("mixed_v")
                    nc.vector.tensor_tensor(by_chunk(bv[:]), by_chunk(bv[:]), out("v"), ALU.mult).then_inc(once["bonus_done"], 1)

KB = [(b * P, min(P, T - b * P)) for b in range(-(-T // P))]
NBLK = len(KB)
NQ = SEQ // P
QB = [META + b * P for b in range(NQ)]
SCORES = [(c, min(512, T - c)) for c in range(0, T, 512)]
LAMBDA_INIT = 0.8 - 0.6
GROUPS = [(0, 4), (4, 8), (8, 9)]
NG = len(GROUPS)


def attention(nc, sems, kept_d, cos_d, sin_d, lambdas, ident, att_d):
    SCALE = DQ ** -0.5
    with ExitStack() as ctx:
        sb = lambda n, s: ctx.enter_context(nc.sbuf_tensor(n, s, F32))
        sem = lambda n: sems.enter_context(nc.semaphore(n))
        lam_v, lam_products = sb("at_lam_v", [P, 4, DQ]), sb("at_lam_products", [P, 2, DQ])
        lam_e, nlam = sb("at_lam_e", [P, 2]), sb("at_nlam", [P, 1])
        cos, sin = sb("at_cos", [P, T]), sb("at_sin", [P, T])
        raw = {x: sb(f"at_{x}", [P, T]) for x in ("q", "q_half", "k", "k_half")}
        vT = sb("at_vT", [P, T])
        part = sb("at_part", [P, T])
        part2 = sb("at_part2", [P, T])
        qR = [sb(f"at_qR{s}", [P, T]) for s in range(2)]
        kR = [sb(f"at_kR{s}", [P, T]) for s in range(2)]
        v = [sb(f"at_v{s}", [P, NBLK, P]) for s in range(2)]
        pr = [[sb(f"at_p{m}{s}", [P, T]) for m in range(2)] for s in range(2)]
        pT = [sb(f"at_pT{s}", [P, NBLK, P]) for s in range(2)]
        mx = [sb(f"at_mx{s}", [P, 2]) for s in range(2)]
        nmx = [sb(f"at_nmx{s}", [P, 2]) for s in range(2)]
        sums = [sb(f"at_sums{s}", [P, 2]) for s in range(2)]
        inv = [sb(f"at_inv{s}", [P, 2]) for s in range(2)]
        coef = [sb(f"at_coef{s}", [P, 1]) for s in range(2)]
        o = [sb(f"at_o{s}", [P, P]) for s in range(2)]
        S = [ctx.enter_context(nc.psum_tensor(f"at_S{m}", [P, 3 * 512], F32)) for m in range(2)]
        tb = ctx.enter_context(nc.psum_tensor("at_tb", [P, 4, P], F32))
        ob = ctx.enter_context(nc.psum_tensor("at_ob", [P, 512], F32))

        tables_here, q_here, k_here, v_here = (sem(f"at_{n}_here") for n in ("tables", "q", "k", "v"))
        lam_here, lam_multiplied, lam_summed, lam_raised, lam_less, lam_done = (sem(f"at_lam_{n}") for n in (
            "here", "multiplied", "summed", "raised", "less", "done"))
        roped = sem("at_roped")
        v_turned, v_kept = sem("at_v_turned"), sem("at_v_kept")
        scored = [sem(f"at_scored{m}") for m in range(2)]
        maxed = [sem(f"at_maxed{m}") for m in range(2)]
        negated = [sem(f"at_negated{m}") for m in range(2)]
        raised = [sem(f"at_raised{m}") for m in range(2)]
        inverted, weighed, combined = sem("at_inverted"), sem("at_weighed"), sem("at_combined")
        turned, copied = sem("at_turned"), sem("at_copied")
        valued, o_scaled = sem("at_valued"), sem("at_o_scaled")
        o_stored = [sem(f"at_o_stored{s}") for s in range(2)]
        LOOP = 4
        STEPS = LOOP * NQ
        done = lambda g: g + STEPS + 1
        group_done = lambda g, j: NG * g + 2 * NG + j + 1

        with nc.Block() as block:
            @block.sync
            def _(sp):
                for sm in (*scored, *maxed, *raised, inverted, weighed, combined, valued, o_scaled):
                    sp.sem_inc(sm, STEPS)
                for sm in (turned, copied):
                    sp.sem_inc(sm, 2 * NG)
                for sm in (v_turned, v_kept):
                    sp.sem_inc(sm, 1)
                sp.sem_inc(roped, 6)
                for s in range(2):
                    sp.sem_inc(o_stored[s], 16)
                sp.dma_start(cos[:], cos_d).then_inc(tables_here, 16)
                sp.dma_start(sin[:], sin_d).then_inc(tables_here, 16)
                half = DQ // 2
                with sp.Fori(0, HEADS) as h:
                    for n, (x, name) in enumerate((("q", "att_q"), ("k", "att_k"))):
                        src = kept_d[KEPT.index(name), h]
                        here = (q_here, k_here)[n]
                        sp.wait_ge(roped, 6 * h + 3 * (n + 1))
                        sp.dma_start(raw[x][:], src).then_inc(here, 16)
                        for quarter in range(4):
                            other = quarter ^ 1
                            sp.dma_start(raw[x + "_half"][quarter * half:(quarter + 1) * half, :],
                                         src[other * half:(other + 1) * half, :]).then_inc(here, 16)
                    sp.wait_ge(v_turned, h + 1)
                    sp.dma_start(vT[:], kept_d[KEPT.index("att_v"), h]).then_inc(v_here, 16)

            @block.gpsimd
            def _(pool):
                pool.wait_ge(tables_here, 32)
                with pool.Fori(0, HEADS // 2) as i:
                    for s in range(2):
                        h = 2 * i + s
                        for n, (x, out) in enumerate((("q", qR[s]), ("k", kR[s]))):
                            pool.wait_ge((q_here, k_here)[n], 80 * h + 80)
                            pool.wait_ge(scored[1], done(NQ * h - NQ - 1))
                            at = 6 * h + 3 * n + 6
                            nc.gpsimd.tensor_tensor(part[:], raw[x][:], cos[:], ALU.mult).then_inc(roped, 1)
                            nc.gpsimd.tensor_tensor(part2[:], raw[x + "_half"][:], sin[:], ALU.mult).then_inc(roped, 1)
                            pool.wait_ge(roped, at + 2)
                            nc.gpsimd.tensor_tensor(out[:], part[:], part2[:], ALU.add).then_inc(roped, 1)
                            pool.wait_ge(roped, at + 3)

            @block.tensor
            def _(pe):
                with pe.Fori(0, HEADS // LOOP) as i:
                    def step(t):
                        return STEPS * i + t

                    def scores(t, m, parts=SCORES):
                        s, q0 = t // NQ % 2, QB[t % NQ]
                        pe.wait_ge(raised[m], done(step(t) - 1))
                        rows = slice(DQ * m, DQ * m + DQ)
                        for c, w in parts:
                            ins = nc.tensor.matmul(S[m][:, c:c + w], qR[s][rows, q0:q0 + P],
                                                   kR[s][rows, c:c + w], start=True, stop=True)
                        if parts[-1] == SCORES[-1]:
                            ins.then_inc(scored[m], 1)

                    def turn_values(t):
                        pe.wait_ge(v_here, 16 * (LOOP * i + t // NQ) + 16)
                        pe.wait_ge(raised[1], done(step(t) - 1))
                        for b, (k0, mk) in enumerate(KB):
                            ins = nc.tensor.transpose(S[1][0:mk, b * P:(b + 1) * P], vT[:, k0:k0 + mk], ident[:])
                        ins.then_inc(v_turned, 1)

                    def turn(t, j):
                        if j == 0:
                            pe.wait_ge(combined, done(step(t)))
                        pe.wait_ge(copied, group_done(step(t), j) - 1)
                        for n, b in enumerate(range(*GROUPS[j])):
                            k0, mk = KB[b]
                            ins = nc.tensor.transpose(tb[0:mk, n, 0:P],
                                                      pr[t % 2][0][:, k0:k0 + mk], ident[:])
                        ins.then_inc(turned, 1)

                    def values(t, j):
                        s, par = t // NQ % 2, t % 2
                        if j == 0:
                            pe.wait_ge(o_scaled, done(step(t) - 1))
                            if t % NQ == 0:
                                pe.wait_ge(v_kept, LOOP * i + t // NQ + 2)
                        pe.wait_ge(copied, group_done(step(t), j))
                        for b in range(*GROUPS[j]):
                            mk = KB[b][1]
                            ins = nc.tensor.matmul(ob[:, 0:P], pT[par][0:mk, b, 0:P], v[s][0:mk, b, :],
                                                   start=(b == 0), stop=(b == NBLK - 1))
                        if j == NG - 1:
                            ins.then_inc(valued, 1)

                    for t in range(STEPS + 1):
                        starts = t < STEPS and t % NQ == 0
                        if starts:
                            pe.wait_ge(roped, 6 * (LOOP * i + t // NQ) + 12)
                        if t < STEPS:
                            scores(t, 0)
                        if starts:
                            turn_values(t)
                            if t > 0:
                                turn(t - 1, 0)
                            pe.wait_ge(v_kept, LOOP * i + t // NQ + 2)
                        if t < STEPS:
                            scores(t, 1, SCORES[:1])
                        if t > 0 and not starts:
                            turn(t - 1, 0)
                        if t < STEPS:
                            scores(t, 1, SCORES[1:])
                        if t > 0:
                            turn(t - 1, 1)
                            values(t - 1, 0)
                            turn(t - 1, 2)
                            values(t - 1, 1)
                            values(t - 1, 2)

            @block.scalar
            def _(act):
                for j, x in enumerate(lambdas):
                    act.dma_start(lam_v[:, j, :], x.broadcast_to([P, DQ])).then_inc(lam_here, 16)
                act.wait_ge(lam_summed, 1)
                nc.scalar.activation(lam_e[:], lam_e[:], ACT.Exp).then_inc(lam_raised, 1)
                with act.Fori(0, HEADS // LOOP) as i:
                    def step(t):
                        return STEPS * i + t

                    def keep_turned(t, j):
                        par = t % 2
                        if j == 0:
                            act.wait_ge(valued, done(step(t) - 2))
                        act.wait_ge(turned, group_done(step(t), j))
                        b0, b1 = GROUPS[j]
                        mk = KB[b0][1]
                        nc.scalar.copy(pT[par][0:mk, b0:b1, 0:P], tb[0:mk, 0:b1 - b0, 0:P]).then_inc(copied, 1)

                    def raise_scores(t, m):
                        par = t % 2
                        if m == 0:
                            act.wait_ge(turned, group_done(step(t) - 2, NG - 1))
                            act.wait_ge(combined, done(step(t) - 2))
                        act.wait_ge(negated[m], step(t) + 1)
                        nc.scalar.activation(pr[par][m][:], S[m][:, 0:T], ACT.Exp,
                                             bias=nmx[par][:, m:m + 1], scale=SCALE,
                                             accum_out=sums[par][:, m:m + 1]).then_inc(raised[m], 1)

                    for t in range(STEPS + 1):
                        if t > 0:
                            keep_turned(t - 1, 0)
                        if t < STEPS:
                            raise_scores(t, 0)
                        if t < STEPS and t % NQ == 0:
                            s = t // NQ % 2
                            act.wait_ge(v_turned, LOOP * i + t // NQ + 2)
                            nc.scalar.copy(v[s][:, 0:NBLK - 1, :].rearrange("p b d -> p (b d)"),
                                           S[1][:, 0:(NBLK - 1) * P])
                            nc.scalar.copy(v[s][0:KB[-1][1], NBLK - 1, :],
                                           S[1][0:KB[-1][1], (NBLK - 1) * P:NBLK * P]).then_inc(v_kept, 1)
                        if t > 0:
                            for j in range(1, NG):
                                keep_turned(t - 1, j)
                        if t < STEPS:
                            raise_scores(t, 1)
                        if t > 0:
                            q0 = QB[(t - 1) % NQ]
                            par = (t - 1) % 2
                            act.wait_ge(o_scaled, done(step(t - 1)))
                            act.dma_start(att_d[q0:q0 + P, bass.ts(LOOP * i + (t - 1) // NQ, P)],
                                          o[par][:]).then_inc(o_stored[par], 16)
                for s in range(2):
                    act.wait_ge(o_stored[s], 16 * NQ * HEADS // 2 + 16)

            @block.vector
            def _(dve):
                dve.wait_ge(lam_here, 64)
                pairs = lam_v[:].rearrange("p (m two) d -> p m two d", two=2)
                nc.vector.tensor_tensor(lam_products[:], pairs[:, :, 0, :], pairs[:, :, 1, :],
                                        ALU.mult).then_inc(lam_multiplied, 1)
                dve.wait_ge(lam_multiplied, 1)
                nc.vector.tensor_reduce(lam_e[:], lam_products[:], AX, ALU.add).then_inc(lam_summed, 1)
                dve.wait_ge(lam_raised, 1)
                nc.vector.tensor_tensor(nlam[:], lam_e[:, 1:2], lam_e[:, 0:1], ALU.subtract).then_inc(lam_less, 1)
                dve.wait_ge(lam_less, 1)
                nc.vector.tensor_scalar(nlam[:], nlam[:], -LAMBDA_INIT, None, ALU.add).then_inc(lam_done, 1)
                dve.wait_ge(lam_done, 1)
                with dve.Fori(0, HEADS // LOOP) as i:
                    def step(t):
                        return STEPS * i + t

                    for t in range(STEPS + 1):
                        par = t % 2
                        if t < STEPS:
                            for m in range(2):
                                dve.wait_ge(scored[m], done(step(t)))
                                dve.wait_ge(raised[m], done(step(t) - 2))
                                nc.vector.tensor_reduce(mx[par][:, m:m + 1], S[m][:, 0:T], AX,
                                                        ALU.max).then_inc(maxed[m], 1)
                                dve.wait_ge(maxed[m], done(step(t)))
                                nc.vector.tensor_scalar(nmx[par][:, m:m + 1], mx[par][:, m:m + 1], -SCALE,
                                                        None, ALU.mult).then_inc(negated[m], 1)
                        if t < STEPS:
                            for m in range(2):
                                dve.wait_ge(raised[m], done(step(t)))
                            nc.vector.reciprocal(inv[par][:], sums[par][:]).then_inc(inverted, 1)
                            dve.wait_ge(inverted, done(step(t)))
                            nc.vector.scalar_tensor_tensor(coef[par][:], inv[par][:, 1:2], nlam[:],
                                                           sums[par][:, 0:1], ALU.mult,
                                                           ALU.mult).then_inc(weighed, 1)
                            dve.wait_ge(weighed, done(step(t)))
                            nc.vector.scalar_tensor_tensor(pr[par][0][:], pr[par][1][:],
                                                           coef[par][:], pr[par][0][:], ALU.mult,
                                                           ALU.add).then_inc(combined, 1)
                        if t > 0:
                            dve.wait_ge(valued, done(step(t - 1)))
                            dve.wait_ge(o_stored[par ^ 1], 8 * (step(t - 1) - (par ^ 1)) + 16)
                            nc.vector.tensor_scalar(o[par ^ 1][:], ob[:, 0:P],
                                                    inv[par ^ 1][:, 0:1], None, ALU.mult).then_inc(o_scaled, 1)

UNITS = 4
LEVELS = [2 ** n for n in range(1, 7)]
NLEV = len(LEVELS)
PAIRS = NT // 2
SLOTS = 5


def joined_columns(ap, size, z):
    groups = L // (2 * size)
    if size > L // 4:
        at = (slice(size, L), slice(0, L - size))[z]
        return ap[:, :, at].unsqueeze(2)
    base = (0, L - groups * 2 * size)[z]
    pairs = ap[:, :, base:base + groups * 2 * size].rearrange("p u (g c) -> p u g c", c=2 * size)
    return pairs[:, :, :, (slice(size, 2 * size), slice(0, size))[z]]


WIDTH = [L - size if size > L // 4 else L // (2 * size) * size for size in LEVELS]
NGROUPS = [1 if size > L // 4 else L // (2 * size) for size in LEVELS]


def recurrence_masks():
    row, col = np.arange(L)[:, None], np.arange(L)[None, :]
    later = [col > row, col < row]
    m_turned = np.stack([np.stack([f, f | (row == col)]) for f in later], 0)

    def join(size):
        at = [(row, col), (L - 1 - row, L - 1 - col)]
        return np.stack([(a // (2 * size) == b // (2 * size)) & (a // size != b // size) for a, b in at], 0)

    first = m_turned[:, 0] & join(1)
    levels = np.stack([m_turned[:, 0] & join(size) for size in LEVELS], 0)
    parts = [m_turned.reshape(4, L, L), first, levels.reshape(2 * NLEV, L, L), (row == col)[None]]
    return np.concatenate(parts, 0).transpose(1, 0, 2).astype(np.float32).copy()


M_TURNED, M_FIRST, M_LEVEL, M_EYE = 0, 4, 6, 6 + 2 * NLEV
NMASK = M_EYE + 1


def pieces():
    out = []
    for p in range(PAIRS):
        a, b = 2 * p, 2 * p + 1
        chain = [(part, k) for k in (a - 2, b - 2) for part in ("chain_w", "chain_u", "chain_s")] if p else []
        ahead = {0: [("raise", a + 2)], 2: [("front", a + 2), ("raise", b + 2)], 4: [("front", b + 2)]}
        if p == PAIRS - 1:
            ahead = {0: [("raise", NT)], 2: [("raise", NT + 1)]}
        for lev in range(NLEV):
            out += [("turn", a, lev), ("turn", b, lev)]
            out += chain[lev:lev + 1]
            out += ahead.get(lev, [])
            out += [("join", a, lev), ("join", b, lev)]
    return out + [("chain_w", NT - 2), ("front", NT), ("chain_u", NT - 2), ("chain_s", NT - 2),
                  ("chain_w", NT - 1), ("front", NT + 1), ("chain_u", NT - 1), ("chain_s", NT - 1)]


PIECES = pieces()
FRONT = ("rows_kb", "rows_v", "mb0", "mb1", "mk0", "mk1", "m")
USES = {"front": FRONT, "chain_w": ("w",), "chain_u": ("u",), "chain_s": ("s", "y")}
SMALL = [(name, piece[1]) for piece in PIECES for name in USES.get(piece[0], ())]
START = [piece for piece in PIECES if piece[0] in ("raise", "front") and piece[1] >= NT]
START_AT = SMALL.index((FRONT[0], NT))
assert len(SMALL) % 2 == 0
NSMALL = len(SMALL) // 2


def recurrence(nc, sems, prep_d, masks_d, ident, y_d):
    with ExitStack() as ctx:
        sb = lambda n, s: ctx.enter_context(nc.sbuf_tensor(n, s, F32))
        sem = lambda n: sems.enter_context(nc.semaphore(n))
        both = lambda name, shape: [[sb(f"rc_{name}{s}{z}", shape) for z in range(2)] for s in range(SLOTS)]
        each = lambda name, shape: [sb(f"rc_{name}{s}", shape) for s in range(SLOTS)]
        masks = sb("rc_masks", [L, NMASK, L])
        rec = both("rec", [P, HALF_REC])
        grow = both("grow", [P, 2, L + 1])
        g_end = both("g_end", [P, 1])
        shrink = both("shrink", [P, L])
        ar = both("ar", [P, 2, 2, L])
        kb = both("kb", [P, 2, L])
        rows = each("rows", [L, 6, P])
        mb = each("mb", [L, 2, 2, 2, L])
        mk = each("mk", [L, 2, 2, 2, L])
        m = each("m", [L, UNITS, L])
        x = each("x", [L, UNITS, L])
        xT = each("xT", [L, UNITS, L])
        wT = each("wT", [L, UNITS * L])
        state = [sb(f"rc_state{s}", [P, 2, P]) for s in range(2)]
        decayed = sb("rc_decayed", [P, 2, P])
        w = sb("rc_w", [L, UNITS, N])
        u = sb("rc_u", [L, UNITS, N])
        y = [sb(f"rc_y{s}", [L, UNITS, N]) for s in range(2)]
        bank = [ctx.enter_context(nc.psum_tensor(f"rc_bank{b}", [P, 512], F32)) for b in range(8)]

        masks_here, zeroed = sem("rc_masks_here"), sem("rc_zeroed")
        rec_here = [sem(f"rc_rec_here{s}") for s in range(SLOTS)]
        raised, spread, decayed_done, x_first = (sem(f"rc_{n}") for n in ("raised", "spread", "decayed", "x_first"))
        state_cleared = sem("rc_state_cleared")
        y_stored = [sem(f"rc_y_stored{s}") for s in range(2)]
        turned = [sem(f"rc_turned{g}") for g in range(2)]
        wT_done = [sem(f"rc_wT_done{g}") for g in range(2)]
        joinedT = [sem(f"rc_joinedT{g}") for g in range(2)]
        xT_done = [sem(f"rc_xT_done{g}") for g in range(2)]
        back = [sem(f"rc_back{g}") for g in range(2)]
        x_done = [sem(f"rc_x_done{g}") for g in range(2)]
        filled = [sem(f"rc_filled{b}") for b in range(2)]
        emptied = [sem(f"rc_emptied{b}") for b in range(2)]

        LC = NLEV * PAIRS

        def step(i, k):
            return NT * i + k + 1 + NT

        def level(i, k, lev):
            return LC * i + NLEV * (k // 2) + lev + 1 + LC

        def small(i, name, k):
            first = 2 if name in FRONT else 0
            n = SMALL.index((name, (k - first) % NT + first))
            return n % 2, NSMALL * (i + (k - first) // NT) + n // 2 + 1 + NSMALL

        def wait_filled(eng, i, name, k):
            b, n = small(i, name, k)
            eng.wait_ge(filled[b], n)
            return bank[6 + b]

        def wait_emptied(eng, i, name, k):
            b, n = small(i, name, k)
            eng.wait_ge(emptied[b], n)

        def units(ap, width):
            return ap[:, 0:UNITS * width].rearrange("p (u w) -> p u w", u=UNITS)

        def grouped(tile, lev):
            return units(tile[0:L, :], WIDTH[lev]).rearrange("p u (g c) -> p u g c", g=NGROUPS[lev])

        def by_direction(ap):
            return ap.rearrange("p (z h) w -> p z h w", z=2)

        def per_head(at):
            return masks[:, at:at + 2, :].unsqueeze(2).broadcast_to([L, 2, 2, L])

        def part(z, name):
            return REC_AT[name if name in REC_AT else name + str(z)] - (z * (REC - HALF_REC))

        head = [slice(N * h, N * h + N) for h in range(2)]
        at_pos = [slice(1, L + 1), slice(0, L)]
        before_pos = [slice(0, L), slice(1, L + 1)]

        def store_y(eng, i, k):
            for z, c in enumerate((k, NT - 1 - k)):
                eng.dma_start(y_d[z, c * L:(c + 1) * L, bass.ts(i, P)],
                              y[k % 2][:, 2 * z:2 * z + 2, :].rearrange("p h v -> p (h v)")).then_inc(y_stored[k % 2], 16)

        with nc.Block() as block:
            @block.sync
            def _(sp):
                for sm in (raised, spread, decayed_done):
                    sp.sem_inc(sm, NT)
                sp.sem_inc(x_first, 2 * NT)
                for g in range(2):
                    sp.sem_inc(y_stored[g], 32)
                    for sm in (turned[g], back[g], x_done[g], wT_done[g], joinedT[g], xT_done[g]):
                        sp.sem_inc(sm, LC)
                    for sm in (filled[g], emptied[g]):
                        sp.sem_inc(sm, (START_AT + 1 - g) // 2)
                sp.dma_start(masks[:], masks_d).then_inc(masks_here, 16)

                def load(i, k, tile, fresh=False):
                    s = k % SLOTS
                    if not fresh:
                        wait_filled(sp, i, "rows_v", k - SLOTS)
                    c = k % NT
                    sp.dma_start(rec[s][0][:], prep_d[tile, c, :, 0:HALF_REC]).then_inc(rec_here[s], 16)
                    sp.dma_start(rec[s][1][:], prep_d[tile, NT - 1 - c, :, REC - HALF_REC:REC]).then_inc(rec_here[s], 16)

                def store(i, k):
                    wait_emptied(sp, i, "y", k)
                    store_y(sp, i, k)

                for k in range(SLOTS):
                    load(0, k, 0, fresh=True)
                with sp.Fori(0, HEADS - 1) as i:
                    for k in range(SLOTS, NT + SLOTS):
                        load(i, k, i + k // NT)
                        if k - SLOTS < NT - 2:
                            store(i, k - SLOTS)
                for k in range(SLOTS, NT + 2):
                    load(HEADS - 1, k, HEADS - 1 if k < NT else 0)
                    store(HEADS - 1, k - SLOTS)
                store(HEADS - 1, NT - 3)

            @block.gpsimd
            def _(pool):
                n = 0
                pool.wait_ge(masks_here, 16)
                pool.wait_ge(zeroed, 4 * SLOTS)
                def work(i, steps):
                    for piece, k, *_ in steps:
                        s = k % SLOTS
                        if piece == "raise":
                            pool.wait_ge(raised, step(i, k))
                            wait_filled(pool, i, "y", k - SLOTS)
                            for z in range(2):
                                src, g = rec[s][z], grow[s][z]
                                for n, (x_name, at) in enumerate((("kk", before_pos[z]), ("r", at_pos[z]))):
                                    o = part(z, x_name)
                                    nc.gpsimd.tensor_tensor(ar[s][z][:, :, n, :],
                                                            src[:, o:o + L].unsqueeze(1).broadcast_to([P, 2, L]),
                                                            g[:, :, at], ALU.mult)
                                o = part(z, "kd")
                                last = nc.gpsimd.tensor_tensor(
                                    kb[s][z][:], src[:, o:o + 2 * L].rearrange("p (a t) -> p a t", a=2),
                                    shrink[s][z][:].unsqueeze(1).broadcast_to([P, 2, L]), ALU.mult)
                            last.then_inc(spread, 1)
                        elif piece == "front":
                            wait_emptied(pool, i, "u", k - SLOTS)
                            for z in range(2):
                                wait_emptied(pool, i, f"mb{z}", k)
                            nc.gpsimd.tensor_tensor(by_direction(xT[s][:]), mb[s][:, :, :, 0, :], per_head(M_FIRST),
                                                    ALU.mult).then_inc(x_first, 1)
                            pool.wait_ge(x_first, 2 * step(i, k) - 1)
                            nc.gpsimd.tensor_tensor(xT[s][:], xT[s][:],
                                                    masks[:, M_EYE:M_EYE + 1, :].broadcast_to([L, UNITS, L]),
                                                    ALU.add).then_inc(x_first, 1)

                work(-1, START)
                with pool.Fori(0, HEADS) as i:
                    work(i, PIECES)

            @block.tensor
            def _(pe):
                pe.wait_ge(masks_here, 16)

                def work(i, steps):
                    def take(name, k):
                        b, n = small(i, name, k)
                        pe.wait_ge(emptied[b], n - 1)
                        return bank[6 + b], filled[b]

                    for piece, k, *lev in steps:
                        s, g = k % SLOTS, k % 2
                        if piece == "front":
                            pe.wait_ge(spread, step(i, k))
                            out, done = take("rows_kb", k)
                            for j in range(4):
                                ins = nc.tensor.transpose(out[0:L, j * P:(j + 1) * P], kb[s][j % 2][:, 1 - j // 2, :], ident[:])
                            ins.then_inc(done, 1)
                            out, done = take("rows_v", k)
                            for z in range(2):
                                o = part(z, "v")
                                ins = nc.tensor.transpose(out[0:L, z * P:(z + 1) * P], rec[s][z][:, o:o + L], ident[:])
                            ins.then_inc(done, 1)
                            for n, name in ((1, "mb"), (0, "mk")):
                                for z in range(2):
                                    out, done = take(f"{name}{z}", k)
                                    nc.tensor.matmul(out[0:L, 0:4 * L], kb[s][z][:, n, :],
                                                     ar[s][z][:].rearrange("p h a t -> p (h a t)"),
                                                     start=True, stop=True).then_inc(done, 1)
                            out, done = take("m", k)
                            for z in range(2):
                                wait_emptied(pe, i, f"mb{z}", k)
                                for h in range(2):
                                    ins = nc.tensor.transpose(units(out[0:L, :], L)[:, 2 * z + h, :],
                                                              mb[s][:, z, h, 0, :], ident[0:L, 0:L])
                            ins.then_inc(done, 1)
                        elif piece == "turn":
                            lev, = lev
                            if lev == 0:
                                pe.wait_ge(x_first, 2 * step(i, k))
                                wait_emptied(pe, i, "m", k)
                            pe.wait_ge(xT_done[g], level(i, k, lev - 1))
                            for j in range(UNITS):
                                ins = nc.tensor.matmul(grouped(bank[3 * g], lev)[:, j, :, :], m[s][:, j, :],
                                                       joined_columns(xT[s][:, j:j + 1, :], LEVELS[lev], j // 2)[:, 0, :, :],
                                                       start=True, stop=True)
                            ins.then_inc(turned[g], 1)
                            for j in range(UNITS):
                                ins = nc.tensor.transpose(units(bank[3 * g + 2][0:L, :], L)[:, j, :], xT[s][:, j, :],
                                                          ident[0:L, 0:L])
                            ins.then_inc(back[g], 1)
                        elif piece == "join":
                            lev, = lev
                            pe.wait_ge(wT_done[g], level(i, k, lev))
                            pe.wait_ge(x_done[g], level(i, k, lev))
                            for j in range(UNITS):
                                ins = nc.tensor.matmul(units(bank[3 * g + 1][0:L, :], WIDTH[lev])[:, j, :], x[s][:, j, :],
                                                       units(wT[s], WIDTH[lev])[:, j, :], start=True, stop=True)
                            ins.then_inc(joinedT[g], 1)
                        elif piece == "chain_w":
                            if k == 0:
                                pe.wait_ge(state_cleared, i + 1)
                            else:
                                wait_emptied(pe, i, "s", k - 1)
                            out, done = take("w", k)
                            for j in range(UNITS):
                                z, h = divmod(j, 2)
                                o = units(out[0:L, :], N)[:, j, :]
                                nc.tensor.matmul(o, ar[s][z][:, h, 0, :], state[g][:, z, head[h]], start=True, stop=False)
                                ins = nc.tensor.matmul(o, mk[s][:, z, h, 0, :], rows[s][:, 4 + z, head[h]],
                                                       start=False, stop=True)
                            ins.then_inc(done, 1)
                        elif piece == "chain_u":
                            wait_emptied(pe, i, "w", k)
                            pe.wait_ge(xT_done[g], level(i, k, NLEV - 1))
                            out, done = take("u", k)
                            for j in range(UNITS):
                                ins = nc.tensor.matmul(units(out[0:L, :], N)[:, j, :], xT[s][:, j, :], w[:, j, :],
                                                       start=True, stop=True)
                            ins.then_inc(done, 1)
                        elif piece == "chain_s":
                            wait_emptied(pe, i, "u", k)
                            out, done = take("s", k)
                            for z in range(2):
                                o = out[:, z * P:(z + 1) * P]
                                nc.tensor.matmul(o, rows[s][:, z, :], u[:, 2 * z:2 * z + 2, :].rearrange("p h v -> p (h v)"),
                                                 start=True, stop=False)
                                ins = nc.tensor.matmul(o, rows[s][:, 2 + z, :], rows[s][:, 4 + z, :], start=False, stop=True)
                            ins.then_inc(done, 1)
                            out, done = take("y", k)
                            for j in range(UNITS):
                                z, h = divmod(j, 2)
                                o = units(out[0:L, :], N)[:, j, :]
                                nc.tensor.matmul(o, ar[s][z][:, h, 1, :], state[g][:, z, head[h]], start=True, stop=False)
                                nc.tensor.matmul(o, mb[s][:, z, h, 1, :], u[:, j, :], start=False, stop=False)
                                ins = nc.tensor.matmul(o, mk[s][:, z, h, 1, :], rows[s][:, 4 + z, head[h]],
                                                       start=False, stop=True)
                            ins.then_inc(done, 1)

                for piece, k in PIECES[PIECES.index(("front", NT)):]:
                    if piece == "front":
                        work(-1, [(piece, k)])
                    else:
                        for name in USES[piece]:
                            b, n = small(-1, name, k)
                            pe.wait_ge(emptied[b], n - 1)
                            pe.sem_inc(filled[b], 1)
                            pe.sem_inc(emptied[b], 1)
                with pe.Fori(0, HEADS) as i:
                    work(i, PIECES)

            @block.scalar
            def _(act):
                def work(i, steps):
                    for piece, k, *lev in steps:
                        s, g = k % SLOTS, k % 2
                        if piece == "raise":
                            act.wait_ge(rec_here[s], 64 * i + 32 * (k // SLOTS) + 32)
                            act.wait_ge(spread, step(i, k - SLOTS))
                            wait_emptied(act, i, "s", k - SLOTS)
                            for z in range(2):
                                o = part(z, "log")
                                sign = (1.0, -1.0)[z]
                                for h in range(2):
                                    nc.scalar.activation(grow[s][z][head[h], h, :], rec[s][z][head[h], o:o + L + 1],
                                                         ACT.Exp, scale=sign)
                                at_end = o + (L, 0)[z]
                                nc.scalar.activation(g_end[s][z][:], rec[s][z][:, at_end:at_end + 1], ACT.Exp, scale=sign)
                                first = o + (1, 0)[z]
                                last = nc.scalar.activation(shrink[s][z][:], rec[s][z][:, first:first + L], ACT.Exp,
                                                            scale=-sign)
                            last.then_inc(raised, 1)
                        elif piece == "front":
                            wait_filled(act, i, "y", k - SLOTS)
                            for name, j0, j1 in (("rows_kb", 0, 4), ("rows_v", 4, 6)):
                                b, _n = small(i, name, k)
                                src = wait_filled(act, i, name, k)
                                nc.scalar.copy(rows[s][:, j0:j1, :].rearrange("p j c -> p (j c)"),
                                               src[0:L, 0:(j1 - j0) * P]).then_inc(emptied[b], 1)
                            b, _n = small(i, "m", k)
                            src = wait_filled(act, i, "m", k)
                            nc.scalar.copy(m[s][:], units(src[0:L, :], L)).then_inc(emptied[b], 1)
                        elif piece == "turn":
                            act.wait_ge(back[g], level(i, k, lev[0]))
                            nc.scalar.copy(x[s][:], units(bank[3 * g + 2][0:L, :], L)).then_inc(x_done[g], 1)
                        elif piece == "chain_w":
                            if k == 0:
                                act.wait_ge(state_cleared, i + 1)
                            else:
                                wait_emptied(act, i, "s", k - 1)
                            for z in range(2):
                                ins = nc.scalar.activation(decayed[:, z, :], state[g][:, z, :], ACT.Copy,
                                                           scale=g_end[s][z][:])
                            ins.then_inc(decayed_done, 1)
                        if piece in ("chain_w", "chain_u"):
                            name, dst = ("w", w) if piece == "chain_w" else ("u", u)
                            b, _n = small(i, name, k)
                            src = wait_filled(act, i, name, k)
                            nc.scalar.copy(dst[:], units(src[0:L, :], N)).then_inc(emptied[b], 1)
                        elif piece == "chain_s":
                            act.wait_ge(y_stored[g], 32 * PAIRS * i + 32 * (k // 2) + 32)
                            b, _n = small(i, "y", k)
                            src = wait_filled(act, i, "y", k)
                            nc.scalar.copy(y[g][:], units(src[0:L, :], N)).then_inc(emptied[b], 1)
                            if k >= NT - 2:
                                wait_emptied(act, i, "y", k)
                                store_y(act, i, k)

                work(-1, START)
                with act.Fori(0, HEADS) as i:
                    work(i, PIECES)
                for g in range(2):
                    act.wait_ge(y_stored[g], 32 * PAIRS * HEADS + 32)

            @block.vector
            def _(dve):
                for s in range(SLOTS):
                    for z in range(2):
                        for h in range(2):
                            nc.vector.memset(grow[s][z][head[1 - h], h, :], 0.0).then_inc(zeroed, 1)
                dve.wait_ge(masks_here, 16)
                def work(i, steps):
                    for piece, k, *lev in steps:
                        s, g = k % SLOTS, k % 2
                        if piece == "front":
                            wait_filled(dve, i, "y", k - SLOTS)
                            for name, dst in (("mb", mb), ("mk", mk)):
                                for z in range(2):
                                    b, _n = small(i, f"{name}{z}", k)
                                    src = wait_filled(dve, i, f"{name}{z}", k)
                                    at = M_TURNED + 2 * z
                                    nc.vector.tensor_tensor(
                                        dst[s][:, z, :, :, :], src[0:L, 0:4 * L].rearrange("p (h a t) -> p h a t", h=2, a=2),
                                        masks[:, at:at + 2, :].unsqueeze(1).broadcast_to([L, 2, 2, L]),
                                        ALU.mult).then_inc(emptied[b], 1)
                        elif piece == "turn":
                            lev, = lev
                            dve.wait_ge(turned[g], level(i, k, lev))
                            for z in range(2):
                                at = M_LEVEL + 2 * lev + z
                                mask = joined_columns(masks[:, at:at + 1, :], LEVELS[lev], z)
                                ins = nc.vector.tensor_tensor(
                                    grouped(wT[s], lev)[:, 2 * z:2 * z + 2], grouped(bank[3 * g], lev)[:, 2 * z:2 * z + 2],
                                    mask.broadcast_to([L, 2, NGROUPS[lev], WIDTH[lev] // NGROUPS[lev]]), ALU.mult)
                            ins.then_inc(wT_done[g], 1)
                        elif piece == "join":
                            lev, = lev
                            dve.wait_ge(joinedT[g], level(i, k, lev))
                            for z in range(2):
                                changed = joined_columns(xT[s][:, 2 * z:2 * z + 2, :], LEVELS[lev], z)
                                ins = nc.vector.tensor_tensor(changed, grouped(bank[3 * g + 1], lev)[:, 2 * z:2 * z + 2],
                                                              changed, ALU.add)
                            ins.then_inc(xT_done[g], 1)
                        elif piece == "chain_s":
                            b, _n = small(i, "s", k)
                            src = wait_filled(dve, i, "s", k)
                            dve.wait_ge(decayed_done, step(i, k))
                            for z in range(2):
                                ins = nc.vector.scalar_tensor_tensor(state[1 - g][:, z, :], src[:, z * P:(z + 1) * P],
                                                                     g_end[s][z][:], decayed[:, z, :], ALU.mult,
                                                                     ALU.add)
                            ins.then_inc(emptied[b], 1)

                work(-1, START)
                with dve.Fori(0, HEADS) as i:
                    wait_filled(dve, i, "y", -1)
                    wait_emptied(dve, i, "s", -1)
                    nc.vector.memset(state[0][:], 0.0).then_inc(state_cleared, 1)
                    work(i, PIECES)

DOWN_EARLY = 12
TOK = SEQ // P
SUBLN_EPS = 1e-5
LNX_EPS = 64e-5


def merge_and_mix(nc, sems, x, att_d, y_d, kept_d, w_out, post_g, ident, table, u2T, h2_d):
    with ExitStack() as ctx:
        sb = lambda n, s: ctx.enter_context(nc.sbuf_tensor(n, s, F32))
        sem = lambda n: sems.enter_context(nc.semaphore(n))
        two = lambda n, s: [sb(f"mm_{n}{p}", s) for p in range(2)]
        wo = sb("mm_wo", [P, KC, D])
        gain = sb("mm_gain", [P, D])
        sub = sb("mm_sub", [P, 1])
        eps = sb("mm_eps", [P, 3])
        att, yf, yb, h = two("att", [P, D]), two("yf", [P, D]), two("yb", [P, D]), two("h", [P, D])
        sq = sb("mm_sq", [P, D])
        sq_y = sb("mm_sq_y", [P, D])
        sq_m = sb("mm_sq_m", [P, D])
        a_st, y_st, m_st = two("a_st", [P, 3, 8]), two("y_st", [P, 4, 16]), two("m_st", [P, 6])
        names = ("g", "bonus_v", "gate_a", "gate_r")
        fm = {n: two(n, [P, KC, P]) for n in names}
        ma, mr, mT = sb("mm_ma", [P, KC, P]), sb("mm_mr", [P, KC, P]), two("mT", [P, KC, P])
        h2, un = two("h2", [P, D]), two("un", [P, D])
        ps = [ctx.enter_context(nc.psum_tensor(f"mm_ps{j}", [P, D], F32)) for j in range(4)]
        ps_a, ps_y, ps_m, ps_u = ps

        consts, const_done = sem("mm_consts"), sem("mm_const_done")
        tok_here = [sem(f"mm_tok_here{p}") for p in range(2)]
        fm_here = [sem(f"mm_fm_here{p}") for p in range(2)]
        x_here = [sem(f"mm_x_here{p}") for p in range(2)]
        h2_stored = [sem(f"mm_h2_stored{p}") for p in range(2)]
        st = {n: sem(f"mm_{n}") for n in (
            "a_squared", "a_summed", "a_rooted", "a_inverse", "a_normed", "a_turned",
            "y_added", "y_summed", "y_mean", "y_centred", "y_squared", "y_varied", "y_rooted", "y_inverse", "y_normed",
            "y_turned", "bonus_shifted", "gated", "ma", "mr_scaled", "mr_shifted", "mr", "merged", "projected",
            "m_squared", "m_rooted", "m_inverse", "m_normed", "h2", "h_squared", "h_rooted", "h_inverse", "u_normed",
            "u_turned", "u_kept")}

        def wait(eng, name, t):
            if t >= 0:
                eng.wait_ge(st[name], t + 1)

        def heads(ap, n):
            return ap.rearrange("p (h c) -> p h c", h=n)

        def columns(name):
            at = PAR[name][0]
            return table[:, at:at + KC].unsqueeze(2).broadcast_to([P, KC, P])

        def tiles(ap):
            return ap.rearrange("p (k t) -> p k t", k=KC)

        STAGES = [(s, t) for step in range(TOK + 4)
                  for s, t in (("turn", step - 4), ("project", step - 2), ("merge", step - 1), ("heads", step),
                               ("norm", step - 3), ("mix", step - 2))
                  if 0 <= t < TOK]

        with nc.Block() as block:
            @block.sync
            def _(sp):
                def load_tokens(t):
                    p = t % 2
                    rows = slice(META + t * P, META + (t + 1) * P)
                    wait(sp, "a_turned", t - 2)
                    wait(sp, "y_turned", t - 2)
                    sp.dma_start(att[p][:], att_d[rows, :]).then_inc(tok_here[p], 16)
                    sp.dma_start(yf[p][:], y_d[0, rows, :]).then_inc(tok_here[p], 16)
                    sp.dma_start(yb[p][:], y_d[1, rows, :]).then_inc(tok_here[p], 16)

                def load_features(t):
                    p = t % 2
                    wait(sp, "merged", t - 2)
                    for n in names:
                        src = kept_d[KEPT.index(n), :, :, META + t * P:META + (t + 1) * P]
                        sp.dma_start(fm[n][p][:], src.rearrange("k p t -> p k t")).then_inc(fm_here[p], 16)

                def load_x(t):
                    p = t % 2
                    wait(sp, "h2", t - 2)
                    sp.dma_start(h[p][:], x[t * P:(t + 1) * P, :]).then_inc(x_here[p], 16)

                load_tokens(0)
                sp.dma_start(gain[:], post_g.broadcast_to([P, D])).then_inc(consts, 16)
                sp.dma_start(wo[:], w_out).then_inc(consts, 16)
                load_features(0)
                for t in range(1, TOK):
                    load_tokens(t)
                    load_features(t)
                    load_x(t - 1)
                load_x(TOK - 1)

            @block.gpsimd
            def _(pool):
                for s, t in STAGES:
                    p = t % 2
                    if s == "heads":
                        pool.wait_ge(tok_here[p], 48 * (t // 2) + 48)
                        nc.gpsimd.tensor_tensor(yf[p][:], yf[p][:], yb[p][:], ALU.add).then_inc(st["y_added"], 1)
                    elif s == "merge":
                        pool.wait_ge(fm_here[p], 64 * (t // 2) + 64)
                        nc.gpsimd.tensor_tensor(fm["bonus_v"][p][:], fm["bonus_v"][p][:], columns("lnx_b"),
                                                ALU.add).then_inc(st["bonus_shifted"], 1)
                        nc.gpsimd.tensor_tensor(fm["g"][p][:], fm["g"][p][:], fm["gate_r"][p][:],
                                                ALU.mult).then_inc(st["gated"], 1)
                    elif s == "mix":
                        wait(pool, "m_normed", t)
                        pool.wait_ge(x_here[p], 16 * (t // 2) + 16)
                        wait(pool, "u_turned", t - 2)
                        if t >= 2:
                            pool.wait_ge(h2_stored[p], 16 * (t // 2))
                        nc.gpsimd.tensor_tensor(h2[p][:], h2[p][:], h[p][:], ALU.add).then_inc(st["h2"], 1)

            @block.tensor
            def _(pe):
                for s, t in STAGES:
                    p = t % 2
                    if s == "heads":
                        for name, src, dst, reader in (("a", att, ps_a, "ma"), ("y", yf, ps_y, "mr_scaled")):
                            wait(pe, f"{name}_normed", t)
                            wait(pe, reader, t - 1)
                            for k in range(KC):
                                ins = nc.tensor.transpose(dst[:, k * P:(k + 1) * P], src[p][:, k * P:(k + 1) * P], ident[:])
                            ins.then_inc(st[f"{name}_turned"], 1)
                    elif s == "project":
                        wait(pe, "merged", t)
                        wait(pe, "m_normed", t - 1)
                        if t == 0:
                            pe.wait_ge(consts, 32)
                        for n in range(2):
                            for k in range(KC):
                                ins = nc.tensor.matmul(ps_m[:, n * 512:(n + 1) * 512], mT[p][:, k, :],
                                                       wo[:, k, n * 512:(n + 1) * 512], start=(k == 0), stop=(k == KC - 1))
                        ins.then_inc(st["projected"], 1)
                    elif s == "turn":
                        wait(pe, "u_normed", t)
                        wait(pe, "u_kept", t - 1)
                        for k in range(KC):
                            ins = nc.tensor.transpose(ps_u[:, k * P:(k + 1) * P], un[p][:, k * P:(k + 1) * P], ident[:])
                        ins.then_inc(st["u_turned"], 1)

            @block.scalar
            def _(act):
                act.wait_ge(const_done, 4)
                for s, t in STAGES:
                    p = t % 2
                    if s == "heads":
                        act.wait_ge(tok_here[p], 48 * (t // 2) + 48)
                        wait(act, "a_summed", t - 1)
                        nc.scalar.activation(sq[:], att[p][:], ACT.Square).then_inc(st["a_squared"], 1)
                        wait(act, "a_summed", t)
                        nc.scalar.activation(a_st[p][:, 1, :], a_st[p][:, 0, :], ACT.Sqrt, bias=eps[:, 0:1],
                                             scale=1.0 / P).then_inc(st["a_rooted"], 1)
                        wait(act, "y_centred", t)
                        nc.scalar.activation(sq_y[:], yf[p][:], ACT.Square).then_inc(st["y_squared"], 1)
                        wait(act, "y_varied", t)
                        nc.scalar.activation(y_st[p][:, 2, :], y_st[p][:, 1, :], ACT.Sqrt, bias=eps[:, 1:2],
                                             scale=1.0 / N).then_inc(st["y_rooted"], 1)
                    elif s == "mix":
                        wait(act, "projected", t)
                        nc.scalar.activation(sq_m[:], ps_m[:], ACT.Square,
                                             accum_out=m_st[p][:, 0:1]).then_inc(st["m_squared"], 1)
                        wait(act, "m_squared", t)
                        nc.scalar.activation(m_st[p][:, 1:2], m_st[p][:, 0:1], ACT.Sqrt, bias=eps[:, 2:3],
                                             scale=1.0 / D).then_inc(st["m_rooted"], 1)
                    elif s == "norm":
                        wait(act, "h2", t)
                        act.dma_start(h2_d[t * P:(t + 1) * P, :], h2[p][:]).then_inc(h2_stored[p], 16)
                        nc.scalar.activation(sq_m[:], h2[p][:], ACT.Square,
                                             accum_out=m_st[p][:, 3:4]).then_inc(st["h_squared"], 1)
                        wait(act, "h_squared", t)
                        nc.scalar.activation(m_st[p][:, 4:5], m_st[p][:, 3:4], ACT.Sqrt, bias=eps[:, 2:3],
                                             scale=1.0 / D).then_inc(st["h_rooted"], 1)
                        wait(act, "h_inverse", t)
                        wait(act, "u_turned", t - 2)
                        nc.scalar.activation(un[p][:], h2[p][:], ACT.Copy,
                                             scale=m_st[p][:, 5:6]).then_inc(st["u_normed"], 1)
                for p in range(2):
                    act.wait_ge(h2_stored[p], 16 * TOK // 2)

            @block.vector
            def _(dve):
                for n, value in enumerate((SUBLN_EPS, LNX_EPS, EPS)):
                    nc.vector.memset(eps[:, n:n + 1], value).then_inc(const_done, 1)
                nc.vector.tensor_scalar(sub[:], table[:, par("subln_g")], 1.0 - LAMBDA_INIT, None,
                                        ALU.mult).then_inc(const_done, 1)
                dve.wait_ge(const_done, 4)
                for s, t in STAGES:
                    p = t % 2
                    if s == "heads":
                        wait(dve, "a_squared", t)
                        nc.vector.tensor_reduce(a_st[p][:, 0, :], heads(sq[:], 8), AX, ALU.add).then_inc(st["a_summed"], 1)
                        wait(dve, "y_added", t)
                        nc.vector.tensor_reduce(y_st[p][:, 0, :], heads(yf[p][:], 16), AX, ALU.add).then_inc(st["y_summed"], 1)
                        wait(dve, "y_summed", t)
                        nc.vector.tensor_scalar(y_st[p][:, 0, :], y_st[p][:, 0, :], 1.0 / N, None,
                                                ALU.mult).then_inc(st["y_mean"], 1)
                        wait(dve, "y_mean", t)
                        nc.vector.tensor_tensor(heads(yf[p][:], 16), heads(yf[p][:], 16),
                                                y_st[p][:, 0, :].unsqueeze(2).broadcast_to([P, 16, N]),
                                                ALU.subtract).then_inc(st["y_centred"], 1)
                        wait(dve, "a_rooted", t)
                        nc.vector.reciprocal(a_st[p][:, 2, :], a_st[p][:, 1, :]).then_inc(st["a_inverse"], 1)
                        wait(dve, "a_inverse", t)
                        nc.vector.tensor_tensor(heads(att[p][:], 8), heads(att[p][:], 8),
                                                a_st[p][:, 2, :].unsqueeze(2).broadcast_to([P, 8, P]),
                                                ALU.mult).then_inc(st["a_normed"], 1)
                        wait(dve, "y_squared", t)
                        nc.vector.tensor_reduce(y_st[p][:, 1, :], heads(sq_y[:], 16), AX, ALU.add).then_inc(st["y_varied"], 1)
                        wait(dve, "y_rooted", t)
                        nc.vector.reciprocal(y_st[p][:, 3, :], y_st[p][:, 2, :]).then_inc(st["y_inverse"], 1)
                        wait(dve, "y_inverse", t)
                        nc.vector.tensor_tensor(heads(yf[p][:], 16), heads(yf[p][:], 16),
                                                y_st[p][:, 3, :].unsqueeze(2).broadcast_to([P, 16, N]),
                                                ALU.mult).then_inc(st["y_normed"], 1)
                    elif s == "merge":
                        wait(dve, "a_turned", t)
                        dve.wait_ge(fm_here[p], 64 * (t // 2) + 64)
                        nc.vector.scalar_tensor_tensor(ma[:], tiles(ps_a[:]), sub[:], fm["gate_a"][p][:], ALU.mult,
                                                       ALU.mult).then_inc(st["ma"], 1)
                        wait(dve, "y_turned", t)
                        nc.vector.tensor_tensor(mr[:], tiles(ps_y[:]), columns("lnx_g"), ALU.mult).then_inc(st["mr_scaled"], 1)
                        wait(dve, "mr_scaled", t)
                        wait(dve, "bonus_shifted", t)
                        nc.vector.tensor_tensor(mr[:], mr[:], fm["bonus_v"][p][:], ALU.add).then_inc(st["mr_shifted"], 1)
                        wait(dve, "mr_shifted", t)
                        wait(dve, "gated", t)
                        nc.vector.tensor_tensor(mr[:], mr[:], fm["g"][p][:], ALU.mult).then_inc(st["mr"], 1)
                        wait(dve, "mr", t)
                        wait(dve, "projected", t - 2)
                        nc.vector.tensor_tensor(mT[p][:], ma[:], mr[:], ALU.add).then_inc(st["merged"], 1)
                    elif s == "mix":
                        wait(dve, "m_rooted", t)
                        nc.vector.reciprocal(m_st[p][:, 2:3], m_st[p][:, 1:2]).then_inc(st["m_inverse"], 1)
                        wait(dve, "m_inverse", t)
                        wait(dve, "u_normed", t - 2)
                        if t >= 2:
                            dve.wait_ge(h2_stored[p], 16 * (t // 2))
                        if t == 0:
                            dve.wait_ge(consts, 32)
                        nc.vector.scalar_tensor_tensor(h2[p][:], ps_m[:], m_st[p][:, 2:3], gain[:], ALU.mult,
                                                       ALU.mult).then_inc(st["m_normed"], 1)
                    elif s == "norm":
                        wait(dve, "h_rooted", t)
                        nc.vector.reciprocal(m_st[p][:, 5:6], m_st[p][:, 4:5]).then_inc(st["h_inverse"], 1)
                    elif s == "turn":
                        wait(dve, "u_turned", t)
                        nc.vector.tensor_tensor(u2T[:, :, t * P:(t + 1) * P], tiles(ps_u[:]), columns("pre_ffn_g"),
                                                ALU.mult).then_inc(st["u_kept"], 1)


HALVES = [(0, 512), (512, 512)]


def ffn_hidden(nc, sems, w_in, w_down, u2T, hidden, down):
    with ExitStack() as ctx:
        sb = lambda n, s: ctx.enter_context(nc.sbuf_tensor(n, s, F32))
        sem = lambda n: sems.enter_context(nc.semaphore(n))
        wt = [[sb(f"fh_w{j}{b}", [P, KC, P]) for b in range(2)] for j in range(2)]
        act_g = [sb(f"fh_act{b}", [P, SEQ]) for b in range(2)]
        ps = [[ctx.enter_context(nc.psum_tensor(f"fh_ps{j}{b}", [P, SEQ], F32)) for b in range(2)] for j in range(2)]
        w_here = [[sem(f"fh_w_here{j}{b}") for b in range(2)] for j in range(2)]
        made = [sem(f"fh_made{j}") for j in range(2)]
        silu_done, hidden_done = sem("fh_silu"), sem("fh_hidden")
        down_here = sem("fh_down_here")
        down_tiles = down.shape[1]

        with nc.Block() as block:
            @block.sync
            def _(sp):
                for sm in (*made, silu_done, hidden_done):
                    sp.sem_inc(sm, 2)
                with sp.Fori(0, FT // 2) as i:
                    for b in range(2):
                        for j in range(2):
                            sp.wait_ge(made[j], 2 * i + b + 1)
                            sp.dma_start(wt[j][b][:], w_in[2 * i + b, j]).then_inc(w_here[j][b], 16)

            @block.gpsimd
            def _(pool):
                pool.dma_start(down[:], w_down[:, 0:down_tiles, :]).then_inc(down_here, 16)
                pool.wait_ge(down_here, 16)

            @block.tensor
            def _(pe):
                with pe.Fori(0, FT // 2) as i:
                    for b in range(2):
                        for j in range(2):
                            pe.wait_ge(w_here[j][b], 16 * i + 16)
                            pe.wait_ge((silu_done, hidden_done)[j], 2 * i + b + 1)
                            for c, width in HALVES:
                                for k in range(KC):
                                    ins = nc.tensor.matmul(ps[j][b][:, c:c + width], wt[j][b][:, k, :], u2T[:, k, c:c + width],
                                                           start=(k == 0), stop=(k == KC - 1))
                            ins.then_inc(made[j], 1)

            @block.scalar
            def _(act):
                with act.Fori(0, FT // 2) as i:
                    for b in range(2):
                        act.wait_ge(made[0], 2 * i + b + 3)
                        act.wait_ge(hidden_done, 2 * i + b + 1)
                        nc.scalar.activation(act_g[b][:], ps[0][b][:], ACT.Silu).then_inc(silu_done, 1)

            @block.vector
            def _(dve):
                with dve.Fori(0, FT // 2) as i:
                    for b in range(2):
                        dve.wait_ge(silu_done, 2 * i + b + 3)
                        dve.wait_ge(made[1], 2 * i + b + 3)
                        nc.vector.tensor_tensor(hidden[:, 2 * i + b, :], ps[1][b][:], act_g[b][:],
                                                ALU.mult).then_inc(hidden_done, 1)


def ffn_down(nc, sems, w_down, h2_d, post_g, hidden, down, space, out):
    with ExitStack() as ctx:
        sb = lambda n, s: ctx.enter_context(nc.sbuf_tensor(n, s, F32))
        sem = lambda n: sems.enter_context(nc.semaphore(n))
        have = down.shape[1]
        more = sb("fd_more", [P, FT - have - KC, D])
        gain = sb("fd_gain", [P, D])
        eps = sb("fd_eps", [P, 1])
        h2 = [sb(f"fd_h2{p}", [P, D]) for p in range(2)]
        f = sb("fd_f", [P, D])
        sq = sb("fd_sq", [P, D])
        st = [sb(f"fd_st{p}", [P, 3]) for p in range(2)]
        ps = [ctx.enter_context(nc.psum_tensor(f"fd_ps{p}", [P, D], F32)) for p in range(2)]
        rest_here, gain_here, eps_set = sem("fd_rest_here"), sem("fd_gain_here"), sem("fd_eps_set")
        h2_here = [sem(f"fd_h2_here{p}") for p in range(2)]
        out_stored = [sem(f"fd_out_stored{p}") for p in range(2)]
        made, squared, rooted, inverse, normed, added = (sem(f"fd_{n}") for n in (
            "made", "squared", "rooted", "inverse", "normed", "added"))

        with nc.Block() as block:
            @block.sync
            def _(sp):
                for k in range(KC):
                    sp.dma_start(space[:, k, :], w_down[:, have + k, :]).then_inc(rest_here, 16)
                sp.dma_start(more[:], w_down[:, have + KC:, :]).then_inc(rest_here, 16)
                sp.dma_start(gain[:], post_g.broadcast_to([P, D])).then_inc(gain_here, 16)
                for t in range(TOK):
                    p = t % 2
                    if t >= 2:
                        sp.wait_ge(out_stored[p], 16 * (t // 2))
                    sp.dma_start(h2[p][:], h2_d[t * P:(t + 1) * P, :]).then_inc(h2_here[p], 16)

            @block.tensor
            def _(pe):
                for t in range(TOK):
                    p = t % 2
                    if t >= 2:
                        pe.wait_ge(normed, t - 1)
                    for k in range(FT):
                        if k == have and t == 0:
                            pe.wait_ge(rest_here, 16 * (KC + 1))
                        w = down[:, k, :] if k < have else space[:, k - have, :] if k < have + KC else more[:, k - have - KC, :]
                        for c, width in HALVES:
                            ins = nc.tensor.matmul(ps[p][:, c:c + width], hidden[:, k, t * P:(t + 1) * P], w[:, c:c + width],
                                                   start=(k == 0), stop=(k == FT - 1))
                    ins.then_inc(made, 1)

            @block.scalar
            def _(act):
                act.wait_ge(eps_set, 1)
                for t in range(TOK):
                    p = t % 2
                    act.wait_ge(made, t + 1)
                    nc.scalar.activation(sq[:], ps[p][:], ACT.Square, accum_out=st[p][:, 0:1]).then_inc(squared, 1)
                    act.wait_ge(squared, t + 1)
                    nc.scalar.activation(st[p][:, 1:2], st[p][:, 0:1], ACT.Sqrt, bias=eps[:], scale=1.0 / D).then_inc(rooted, 1)
                    act.wait_ge(added, t + 1)
                    act.dma_start(out[t * P:(t + 1) * P, :], h2[p][:]).then_inc(out_stored[p], 16)
                for p in range(2):
                    act.wait_ge(out_stored[p], 16 * TOK // 2)

            @block.vector
            def _(dve):
                nc.vector.memset(eps[:], EPS).then_inc(eps_set, 1)
                dve.wait_ge(gain_here, 16)
                for t in range(TOK):
                    p = t % 2
                    dve.wait_ge(rooted, t + 1)
                    nc.vector.reciprocal(st[p][:, 2:3], st[p][:, 1:2]).then_inc(inverse, 1)
                    dve.wait_ge(inverse, t + 1)
                    if t >= 1:
                        dve.wait_ge(added, t)
                    nc.vector.scalar_tensor_tensor(f[:], ps[p][:], st[p][:, 2:3], gain[:], ALU.mult, ALU.mult).then_inc(normed, 1)
                    dve.wait_ge(normed, t + 1)
                    dve.wait_ge(h2_here[p], 16 * (t // 2) + 16)
                    nc.vector.tensor_tensor(h2[p][:], f[:], h2[p][:], ALU.add).then_inc(added, 1)


def tail(nc, sems, space, a, att_d, y_d, kept_d, h2_d, ident, table):
    sb = lambda n, s: space.enter_context(nc.sbuf_tensor(n, s, F32))
    u2T = sb("u2T", [P, KC, SEQ])
    merge_and_mix(nc, sems, a["x"], att_d, y_d, kept_d, a["w_out"], a["post_mix_g"], ident, table, u2T, h2_d)
    hidden, down = sb("hidden", [P, FT, SEQ]), sb("down", [P, DOWN_EARLY, D])
    ffn_hidden(nc, sems, a["w_ffn_in"], a["w_ffn_out"], u2T, hidden, down)
    ffn_down(nc, sems, a["w_ffn_out"], h2_d, a["post_ffn_g"], hidden, down, u2T, a["out"])


class fresh_semaphores:

    def __init__(self, nc):
        self.nc, self.taken = nc, []

    def __enter__(self):
        return self

    def enter_context(self, context):
        handle = context.__enter__()
        self.taken.append(handle)
        return handle

    def __exit__(self, *error):
        if error[0] is None:
            self.nc.clear_and_free_semaphores(self.taken)
            self.nc.all_engine_barrier()


def build(nc, a):
    dram = lambda name, shape: nc.dram_tensor(name, shape, F32).ap()
    prep_d = dram("s_prep", [HEADS, NT, P, REC])
    kept_d = dram("s_kept", [len(KEPT), HEADS, P, T])
    att_d = dram("s_att", [T, D])
    y_d = dram("s_y", [2, T, D])
    h2_d = dram("s_h2", [SEQ, D])
    with ExitStack() as whole:
        sb = lambda where, n, s: where.enter_context(nc.sbuf_tensor(n, s, F32))
        ident, ones = sb(whole, "ident", [P, P]), sb(whole, "ones", [P, P])
        table, more = sb(whole, "table", [P, NPAR]), sb(whole, "more", [P, 94])
        with fresh_semaphores(nc) as sems:
            load_constants(nc, sems, a["ident"], a["ones"], a["params"], ident, ones, table, more)
            with ExitStack() as part:
                uT = sb(part, "uT", [P, KC, T])
                lor, gl, gl2 = sb(part, "lor", [P, T]), sb(part, "gl", [P, T]), sb(part, "gl2", [GL - P, T])
                norm_and_turn(nc, sems, a["meta_tokens"], a["x"], ident, table, uT)
                low_rank_inputs(nc, sems, a["w_lora"], uT, more, lor, gl, gl2)
                project_and_prepare(nc, sems, a["w_main"], a["w_low"], uT, ones, table, more, lor, gl, gl2, prep_d, kept_d)
        with fresh_semaphores(nc) as sems:
            lambdas = [a[n] for n in ("lq1", "lk1", "lq2", "lk2")]
            attention(nc, sems, kept_d, a["cos"], a["sin"], lambdas, ident, att_d)
            recurrence(nc, sems, prep_d, a["masks"], ident, y_d)
        tail(nc, whole, whole, a, att_d, y_d, kept_d, h2_d, ident, table)


def kernel(x, meta_tokens, pre_mix_g, w_in, att_lq1, att_lk1, att_lq2, att_lk2, att_subln_g, rwkv_mu, rwkv_w0,
           rwkv_w_up, rwkv_a0, rwkv_a_up, rwkv_g_up, rwkv_k_k, rwkv_k_a, rwkv_r_k, rwkv_lnx_g, rwkv_lnx_b, w_out,
           post_mix_g, pre_ffn_g, w_ffn_in, w_ffn_out, post_ffn_g):
    import concourse.bacc as bacc
    from concourse.bass_utils import run_bass_kernel_spmd

    arr = lambda v: np.asarray(v)[0]
    w = arr(w_in)

    def feature_tiles(m, first, n):
        return m[:, first:first + n * P].reshape(-1, P, n, P).transpose(2, 1, 0, 3)

    starts = {"r": RW0, "k": RW0 + D, "v": RW0 + 2 * D, "att_q": 0, "att_k": D, "att_v": 2 * D, "gate_a": GATE0,
              "gate_r": GATE0 + D}
    w_main = np.stack([feature_tiles(w, starts[n], HEADS) for n in MAIN], 1)
    w_lora = w[:, LORA0:GATE0].reshape(KC, P, GATE0 - LORA0).transpose(1, 0, 2)
    w_low = np.zeros((HEADS, P, 6, P), w.dtype)
    w_up = arr(rwkv_w_up).reshape(2, N, HEADS, P)
    a_up = arr(rwkv_a_up).reshape(2, N, HEADS, P)
    g_up = arr(rwkv_g_up).reshape(GL, HEADS, P)
    for z in range(2):
        w_low[:, :N, z] = w_up[z].transpose(1, 0, 2)
        w_low[:, N:, 2 + z] = a_up[z].transpose(1, 0, 2)
    w_low[:, :, 4] = g_up[:P].transpose(1, 0, 2)
    w_low[:, :GL - P, 5] = g_up[P:].transpose(1, 0, 2)
    columns = lambda v: np.reshape(v, (-1, P)).T
    mu = arr(rwkv_mu)
    mu_lora = np.zeros(3 * P, mu.dtype)
    mu_lora[:GATE0 - LORA0] = mu[3 * D:]
    params = np.concatenate([columns(v) for v in (
        mu[:3 * D], mu_lora, arr(rwkv_w0), arr(rwkv_a0), arr(rwkv_k_k), arr(rwkv_k_a), arr(rwkv_r_k), arr(rwkv_lnx_g),
        arr(rwkv_lnx_b), arr(pre_mix_g), arr(post_mix_g), arr(pre_ffn_g), arr(post_ffn_g), arr(att_subln_g))], 1)
    inv = (1.0 / (np.float32(10000.0) ** (np.arange(0, DQ, 2, dtype=np.float32) / np.float32(DQ)))).astype(np.float32)
    angle = np.arange(T, dtype=np.float32)[None, :] * inv[:, None]
    cos, sin = np.cos(angle), np.sin(angle)
    w1 = arr(w_ffn_in)
    ffn_in = np.stack([feature_tiles(w1, 0, FT), feature_tiles(w1, FFN, FT)], 1)
    arrays = {
        "x": np.asarray(x)[0], "meta_tokens": np.asarray(meta_tokens), "w_main": w_main, "w_lora": w_lora,
        "w_low": w_low, "params": params, "ident": np.eye(P, dtype=np.float32),
        "ones": np.kron(np.eye(2, dtype=np.float32), np.ones((N, N), np.float32)), "masks": recurrence_masks(),
        "lq1": np.asarray(att_lq1), "lk1": np.asarray(att_lk1), "lq2": np.asarray(att_lq2), "lk2": np.asarray(att_lk2),
        "cos": np.concatenate([cos] * 4, 0), "sin": np.concatenate([-sin, sin, -sin, sin], 0),
        "w_out": arr(w_out).reshape(KC, P, D).transpose(1, 0, 2), "post_mix_g": np.asarray(post_mix_g),
        "w_ffn_in": ffn_in, "w_ffn_out": arr(w_ffn_out).reshape(FT, P, D).transpose(1, 0, 2),
        "post_ffn_g": np.asarray(post_ffn_g),
    }
    nc = bacc.Bacc("TRN2", target_bir_lowering=False, num_devices=1)
    ins, aps = {}, {}
    for name, v in arrays.items():
        v = np.ascontiguousarray(v)
        ins[f"in_{name}"] = v
        aps[name] = nc.dram_tensor(f"in_{name}", v.shape, mybir.dt.from_np(v.dtype), kind="ExternalInput").ap()
    aps["out"] = nc.dram_tensor("out_0", [SEQ, D], F32, kind="ExternalOutput").ap()
    build(nc, aps)
    result = run_bass_kernel_spmd(nc, [ins], core_ids=[0])
    return result.results[0]["out_0"].reshape(1, SEQ, D)
```
